# Optimizing a Trainium2 kernel written in Bass

```python
import jax, jax.numpy as jnp
from jax import lax
import numpy as np
import math

D_MODEL = 1024
BATCH = 1
SEQ = 512
DEPTH = 2

N_META = 16
D_MIX = D_MODEL
D_CONV = D_MIX // 2
CONV_WIDTH = 31
N_HEADS = 8
HEAD_DIM = 64
D_ATTN = N_HEADS * HEAD_DIM
N_IDX_HEADS = 8
IDX_DIM = 64
TOPK_MAX = 256
ROPE_THETA = 10000.0
Q_BLOCK = 64
POS_BLOCK = 128
LN_EPS = 1e-5
IDX_SCALE = IDX_DIM ** -0.5
IDX_W_SCALE = N_IDX_HEADS ** -0.5
DEEPNORM_ALPHA = (2.0 * DEPTH) ** 0.25
DEEPNORM_BETA = (8.0 * DEPTH) ** -0.25

IN_SIZES = [D_CONV, D_CONV, D_CONV, D_ATTN, D_ATTN, D_ATTN, D_ATTN,
            N_IDX_HEADS * IDX_DIM, IDX_DIM, N_IDX_HEADS]
D_IN = sum(IN_SIZES)
IN_SPLITS = [sum(IN_SIZES[:i + 1]) for i in range(len(IN_SIZES) - 1)]


def layer_norm(x, g, b):
    xf = x.astype(jnp.float32)
    mu = jnp.mean(xf, axis=-1, keepdims=True)
    var = jnp.mean(jnp.square(xf - mu), axis=-1, keepdims=True)
    y = (xf - mu) * lax.rsqrt(var + LN_EPS) * g.astype(jnp.float32) + b.astype(jnp.float32)
    return y.astype(x.dtype)

def rope_tables(length, dim):
    inv_freq = ROPE_THETA ** (-jnp.arange(0, dim, 2, dtype=jnp.float32) / dim)
    ang = jnp.arange(length, dtype=jnp.float32)[:, None] * inv_freq[None, :]
    return jnp.cos(ang), jnp.sin(ang)

def apply_rope(x, cos, sin):
    half = x.shape[-1] // 2
    x1, x2 = x[..., :half], x[..., half:]
    out = jnp.concatenate([x1 * cos - x2 * sin, x2 * cos + x1 * sin], axis=-1)
    return out.astype(x.dtype)

def conformer_conv_branch(a, g, z, w_dw, b_dw, ln_g, ln_b):
    u = a * jax.nn.sigmoid(g)
    u = lax.conv_general_dilated(
        u, w_dw[:, None, :].astype(u.dtype), window_strides=(1,),
        padding=[(CONV_WIDTH - 1, 0)],
        dimension_numbers=('NWC', 'WIO', 'NWC'),
        feature_group_count=D_CONV) + b_dw
    u = jax.nn.silu(layer_norm(u, ln_g, ln_b))
    return u * jax.nn.silu(z)

def dsa_sparse_attention(q, k, v, qi, ki, wi, topk):
    B, L = q.shape[0], q.shape[1]
    nb = L // Q_BLOCK
    key_pos = jnp.arange(L)
    ki32 = ki.astype(jnp.float32)

    def to_blocks(t):
        return jnp.moveaxis(t.reshape((B, nb, Q_BLOCK) + t.shape[2:]), 1, 0)

    def one_block(args):
        qb, qib, wib, start = args
        q_pos = start + jnp.arange(Q_BLOCK)
        causal = key_pos[None, :] <= q_pos[:, None]
        logits = jnp.einsum('bqhd,bsd->bqhs', qib.astype(jnp.float32), ki32) * IDX_SCALE
        score = jnp.einsum('bqhs,bqh->bqs', jax.nn.relu(logits),
                           wib.astype(jnp.float32) * IDX_W_SCALE)
        score = jnp.where(causal[None], score, -jnp.inf)
        _, idx = lax.top_k(score, topk)
        valid = idx <= q_pos[None, :, None]
        kg = jax.vmap(lambda kk, ii: kk[ii])(k, idx)
        vg = jax.vmap(lambda vv, ii: vv[ii])(v, idx)
        s = jnp.einsum('bqhd,bqkhd->bqhk', qb, kg).astype(jnp.float32) * (HEAD_DIM ** -0.5)
        s = jnp.where(valid[:, :, None, :], s, -jnp.inf)
        p = jax.nn.softmax(s, axis=-1).astype(v.dtype)
        return jnp.einsum('bqhk,bqkhd->bqhd', p, vg)

    starts = jnp.arange(nb) * Q_BLOCK
    out = lax.map(one_block, (to_blocks(q), to_blocks(qi), to_blocks(wi), starts))
    return jnp.moveaxis(out, 0, 1).reshape(B, L, D_ATTN)

def first_inputs(seed: int = 0) -> dict:
    key = jax.random.key(seed)
    ks = jax.random.split(key, 10)
    f32 = jnp.float32
    x = jax.random.normal(ks[0], (BATCH, SEQ, D_MODEL), f32)
    meta_tokens = jax.random.normal(ks[1], (N_META, D_MODEL), f32)
    w_in = jax.random.normal(ks[2], (DEPTH, D_MODEL, D_IN), f32) * D_MODEL ** -0.5
    conv_w = jax.random.normal(ks[3], (DEPTH, CONV_WIDTH, D_CONV), f32) * CONV_WIDTH ** -0.5
    conv_b = 0.01 * jax.random.normal(ks[4], (DEPTH, D_CONV), f32)
    conv_ln_g = 1.0 + 0.01 * jax.random.normal(ks[5], (DEPTH, D_CONV), f32)
    conv_ln_b = 0.01 * jax.random.normal(ks[6], (DEPTH, D_CONV), f32)
    w_out = jax.random.normal(ks[7], (DEPTH, D_MIX, D_MODEL), f32) * (D_MIX ** -0.5) * DEEPNORM_BETA
    post_ln_g = 1.0 + 0.01 * jax.random.normal(ks[8], (DEPTH, D_MODEL), f32)
    post_ln_b = 0.01 * jax.random.normal(ks[9], (DEPTH, D_MODEL), f32)
    return {"x": x, "meta_tokens": meta_tokens, "w_in": w_in, "conv_w": conv_w,
            "conv_b": conv_b, "conv_ln_g": conv_ln_g, "conv_ln_b": conv_ln_b,
            "w_out": w_out, "post_ln_g": post_ln_g, "post_ln_b": post_ln_b}

def first_block(x, meta_tokens, w_in, conv_w, conv_b, conv_ln_g, conv_ln_b, w_out,
              post_ln_g, post_ln_b):
    B, S, D = x.shape
    L = S + N_META
    topk = min(TOPK_MAX, L // 4)
    Lp = -(-L // POS_BLOCK) * POS_BLOCK
    meta = jnp.broadcast_to(meta_tokens[None].astype(x.dtype), (B, N_META, D))
    h = jnp.concatenate([meta, x, jnp.zeros((B, Lp - L, D), x.dtype)], axis=1)
    cos, sin = rope_tables(Lp, HEAD_DIM)
    cos_h, sin_h = cos[:, None, :], sin[:, None, :]

    for l in range(DEPTH):
        proj = jnp.einsum('bld,de->ble', h, w_in[l])
        a, g, zc, q, k, v, za, qi, ki, wi = jnp.split(proj, IN_SPLITS, axis=-1)
        y_conv = conformer_conv_branch(a, g, zc, conv_w[l], conv_b[l], conv_ln_g[l], conv_ln_b[l])
        q = apply_rope(q.reshape(B, Lp, N_HEADS, HEAD_DIM), cos_h, sin_h)
        k = apply_rope(k.reshape(B, Lp, N_HEADS, HEAD_DIM), cos_h, sin_h)
        v = v.reshape(B, Lp, N_HEADS, HEAD_DIM)
        qi = apply_rope(qi.reshape(B, Lp, N_IDX_HEADS, IDX_DIM), cos_h, sin_h)
        ki = apply_rope(ki, cos, sin)
        y_attn = dsa_sparse_attention(q, k, v, qi, ki, wi, topk) * jax.nn.silu(za)
        y = jnp.einsum('ble,ed->bld', jnp.concatenate([y_conv, y_attn], axis=-1), w_out[l])
        h = layer_norm(DEEPNORM_ALPHA * h + y, post_ln_g[l], post_ln_b[l])

    return h[:, N_META:L]


DEPTH_2 = 1

GRID_W = 64
N_Q_HEADS = 8
N_KV_HEADS = 2
GQA_GROUP = N_Q_HEADS // N_KV_HEADS
ATTN_WIDTH = N_Q_HEADS * HEAD_DIM
KV_WIDTH = N_KV_HEADS * HEAD_DIM
Q_BLOCK_2 = 128
AXIAL_DIM = HEAD_DIM // 2
CHUNK = 128
N_GROUPS = 8
GMLP_WIDTH = 512
GROUP_DIM = GMLP_WIDTH // N_GROUPS
N_BRANCHES = 2
EPS = 1e-6

IN_SIZES_2 = (ATTN_WIDTH, KV_WIDTH, KV_WIDTH, ATTN_WIDTH,
            GMLP_WIDTH, GMLP_WIDTH, GMLP_WIDTH, N_BRANCHES * D_MODEL)
IN_WIDTH = sum(IN_SIZES_2)
IN_SPLITS_2 = tuple(int(s) for s in np.cumsum(IN_SIZES_2)[:-1])


def rmsnorm(x, gain):
    x32 = x.astype(jnp.float32)
    y = x32 * lax.rsqrt(jnp.mean(x32 * x32, axis=-1, keepdims=True) + EPS)
    return (y * gain.astype(jnp.float32)).astype(x.dtype)

def layernorm(x, gain, bias):
    x32 = x.astype(jnp.float32)
    mu = jnp.mean(x32, axis=-1, keepdims=True)
    var = jnp.mean(jnp.square(x32 - mu), axis=-1, keepdims=True)
    y = (x32 - mu) * lax.rsqrt(var + EPS)
    return (y * gain.astype(jnp.float32) + bias.astype(jnp.float32)).astype(x.dtype)

def rope_half(x, ang):
    n = x.shape[-1] // 2
    x1, x2 = x[..., :n], x[..., n:]
    cos, sin = jnp.cos(ang).astype(x.dtype), jnp.sin(ang).astype(x.dtype)
    return jnp.concatenate([x1 * cos - x2 * sin, x1 * sin + x2 * cos], axis=-1)

def axial_rope(x, row_ang, col_ang):
    return jnp.concatenate([rope_half(x[..., :AXIAL_DIM], row_ang),
                            rope_half(x[..., AXIAL_DIM:], col_ang)], axis=-1)

def block_attention(q, k, v):
    B, S = q.shape[0], q.shape[1]
    n_blk = S // Q_BLOCK_2
    scale = 1.0 / math.sqrt(HEAD_DIM)
    qb = q.reshape(B, n_blk, Q_BLOCK_2, N_KV_HEADS, GQA_GROUP, HEAD_DIM).transpose(1, 0, 3, 4, 2, 5)
    kt = k.transpose(0, 2, 1, 3)
    vt = v.transpose(0, 2, 1, 3)

    def one_block(q_blk):
        s = jnp.einsum('bhgqd,bhkd->bhgqk', q_blk, kt).astype(jnp.float32) * scale
        p = jax.nn.softmax(s, axis=-1).astype(vt.dtype)
        return jnp.einsum('bhgqk,bhkd->bhgqd', p, vt)

    o = lax.map(one_block, qb)
    return o.transpose(1, 0, 4, 2, 3, 5).reshape(B, S, ATTN_WIDTH)

def hybrid_layer(x, norm_gain, w_in, q_gain, k_gain, w_proj_attn,
                 ln_v_gain, ln_v_bias, w_spatial, b_spatial, w_proj_gmlp,
                 b_merge, w_out):
    B, S, _ = x.shape
    rows = S // GRID_W
    h = rmsnorm(x, norm_gain)
    z = jnp.einsum('bsd,de->bse', h, w_in)
    q, k, v, gate_a, u_in, v_in, gate_b, g_merge = jnp.split(z, IN_SPLITS_2, axis=-1)

    row_idx = jnp.repeat(jnp.arange(rows, dtype=jnp.float32), GRID_W)
    col_idx = jnp.tile(jnp.arange(GRID_W, dtype=jnp.float32), rows)
    inv_freq = ROPE_THETA ** (-jnp.arange(0, AXIAL_DIM, 2, dtype=jnp.float32) / AXIAL_DIM)
    row_ang = (row_idx[:, None] * inv_freq)[:, None, :]
    col_ang = (col_idx[:, None] * inv_freq)[:, None, :]
    q = axial_rope(rmsnorm(q.reshape(B, S, N_Q_HEADS, HEAD_DIM), q_gain), row_ang, col_ang)
    k = axial_rope(rmsnorm(k.reshape(B, S, N_KV_HEADS, HEAD_DIM), k_gain), row_ang, col_ang)
    v = v.reshape(B, S, N_KV_HEADS, HEAD_DIM)
    attn = block_attention(q, k, v) * jax.nn.silu(gate_a)
    y_a = jnp.einsum('bse,ed->bsd', attn, w_proj_attn)

    u = jax.nn.gelu(u_in)
    vv = layernorm(jax.nn.gelu(v_in), ln_v_gain, ln_v_bias)
    vv = vv.reshape(B, S // CHUNK, CHUNK, N_GROUPS, GROUP_DIM)
    v_mix = jnp.einsum('gij,bcjgd->bcigd', w_spatial, vv) + b_spatial.T[:, :, None]
    gm = u * v_mix.reshape(B, S, GMLP_WIDTH) * jax.nn.silu(gate_b)
    y_b = jnp.einsum('bse,ed->bsd', gm, w_proj_gmlp)

    g = jax.nn.sigmoid(g_merge.reshape(B, S, N_BRANCHES, D_MODEL) + b_merge)
    y = g[:, :, 0, :] * y_a + g[:, :, 1, :] * y_b
    return x + jnp.einsum('bsd,de->bse', y, w_out)

def second_inputs(seed: int = 0) -> dict:
    key = jax.random.key(seed)
    ks = jax.random.split(key, 16)
    L = DEPTH_2
    nrm = lambda k, shape, fan: jax.random.normal(k, shape, jnp.float32) * (fan ** -0.5)
    return {
        "x": jax.random.normal(ks[0], (BATCH, SEQ, D_MODEL), jnp.float32),
        "norm_gain": 1.0 + 0.05 * jax.random.normal(ks[1], (L, D_MODEL), jnp.float32),
        "w_in": nrm(ks[2], (L, D_MODEL, IN_WIDTH), D_MODEL),
        "q_gain": 1.0 + 0.05 * jax.random.normal(ks[3], (L, HEAD_DIM), jnp.float32),
        "k_gain": 1.0 + 0.05 * jax.random.normal(ks[4], (L, HEAD_DIM), jnp.float32),
        "w_proj_attn": nrm(ks[5], (L, ATTN_WIDTH, D_MODEL), ATTN_WIDTH),
        "ln_v_gain": 1.0 + 0.05 * jax.random.normal(ks[6], (L, GMLP_WIDTH), jnp.float32),
        "ln_v_bias": 0.02 * jax.random.normal(ks[7], (L, GMLP_WIDTH), jnp.float32),
        "w_spatial": nrm(ks[8], (L, N_GROUPS, CHUNK, CHUNK), CHUNK),
        "b_spatial": 1.0 + 0.05 * jax.random.normal(ks[9], (L, N_GROUPS, CHUNK), jnp.float32),
        "w_proj_gmlp": nrm(ks[10], (L, GMLP_WIDTH, D_MODEL), GMLP_WIDTH),
        "b_merge": 0.02 * jax.random.normal(ks[11], (L, N_BRANCHES, D_MODEL), jnp.float32),
        "w_out": nrm(ks[12], (L, D_MODEL, D_MODEL), D_MODEL),
        "final_gain": 1.0 + 0.05 * jax.random.normal(ks[13], (D_MODEL,), jnp.float32),
    }

def second_block(x, norm_gain, w_in, q_gain, k_gain, w_proj_attn, ln_v_gain, ln_v_bias,
              w_spatial, b_spatial, w_proj_gmlp, b_merge, w_out, final_gain):
    for l in range(DEPTH_2):
        x = hybrid_layer(x, norm_gain[l], w_in[l], q_gain[l], k_gain[l], w_proj_attn[l],
                         ln_v_gain[l], ln_v_bias[l], w_spatial[l], b_spatial[l],
                         w_proj_gmlp[l], b_merge[l], w_out[l])
    return rmsnorm(x, final_gain)


def setup_inputs(seed=0):
    out = dict(first_inputs(seed))
    for name, value in second_inputs(seed + 1).items():
        if name != "x":
            out[name + "_2"] = value
    return out


def reference(
    x, meta_tokens, w_in, conv_w, conv_b, conv_ln_g, conv_ln_b, w_out, post_ln_g, post_ln_b,
    norm_gain_2, w_in_2, q_gain_2, k_gain_2, w_proj_attn_2, ln_v_gain_2, ln_v_bias_2,
    w_spatial_2, b_spatial_2, w_proj_gmlp_2, b_merge_2, w_out_2, final_gain_2,
):
    x = first_block(
        x, meta_tokens, w_in, conv_w, conv_b, conv_ln_g, conv_ln_b, w_out, post_ln_g, post_ln_b,
    )
    return second_block(
        x, norm_gain_2, w_in_2, q_gain_2, k_gain_2, w_proj_attn_2, ln_v_gain_2, ln_v_bias_2,
        w_spatial_2, b_spatial_2, w_proj_gmlp_2, b_merge_2, w_out_2, final_gain_2,
    )


_drawn_inputs = setup_inputs


def setup_inputs(seed=0):
    import zlib

    import numpy as np

    out = dict(_drawn_inputs(seed))
    spreads = {}
    factors = {'conv_b': 8.0,
     'conv_ln_g': 8.0,
     'conv_ln_b': 8.0,
     'post_ln_g': 3.804,
     'post_ln_b': 3.414,
     'q_gain_2': 22.035,
     'k_gain_2': 8.0,
     'ln_v_gain_2': 23.06,
     'ln_v_bias_2': 57.509,
     'b_spatial_2': 22.08,
     'b_merge_2': 8.0}
    for name, (base, spread) in spreads.items():
        noise = np.random.default_rng([zlib.crc32(name.encode()), seed]).standard_normal(out[name].shape)
        drawn = base * np.exp(spread * noise) if base else spread * noise
        out[name] = __import__('jax').numpy.asarray(drawn.astype(out[name].dtype))
    for name, factor in factors.items():
        out[name] = (out[name] * factor).astype(out[name].dtype)
    return out
```

```python
from contextlib import ExitStack

import numpy as np

import concourse.bass as bass
from concourse import mybir

ALU = mybir.AluOpType
ACT = mybir.ActivationFunctionType
F32 = mybir.dt.float32
F32R = mybir.dt.float32r
BF16 = mybir.dt.bfloat16

P = 128
D = 1024
KD = D // P
SEQ = 512
META = 16
L = META + SEQ
PAD = 30
TAPS = PAD + 1
DC = 512
CT = DC // P
HEADS = 8
HD = 64
TOPK = 132
DEPTH = 2
ALPHA = (2.0 * DEPTH) ** 0.25
LN_EPS = 1e-5
EPS = 1e-6
SCALE = HD ** -0.5
IDX_SCALE = HD ** -0.5
IDX_W_SCALE = HEADS ** -0.5
THETA = 10000.0
GRID_W = 64
AXIAL = HD // 2
GROUPS = 8
GD = DC // GROUPS

START = [0, 16, 144, 272, 400]
SIZE = [16, 128, 128, 128, 128]
END = [s + n for s, n in zip(START, SIZE)]
TILES = range(5)
MAIN = range(1, 5)
SCORE_AT = [None, 0, 144, 416, 816]
SCORES = 816 + END[4]
MASK0_AT = SCORES

FILL = -3.0e38
MARK = -3.3e38
HIDE = -1.0e30

BLOCK = 2048
RING = 3
RAWS = 2
PASSES = ((0, 0), (0, 1), (1, 0))


def query_tiles(l):
    return TILES if l == 0 else MAIN


def column_halves(first):
    mid = first + (L - first) // 2
    return (first, mid), (mid, L)


def weight_blocks():
    out = []
    for l in range(DEPTH):
        t_last = 4
        for name, c in (("a", 0), ("g", 0), ("a", 2), ("g", 2), ("qi", 0), ("qi", 2)):
            out.append(((l, name, c), BLOCK, (l, name, c + 1)))
        out.append(((l, "ki", 0), KD * (HD + HEADS), (l, "ki", 0)))
        for name, c in (("zc", 0), ("q", 0), ("q", 2), ("k", 0), ("k", 2), ("zc", 2)):
            out.append(((l, name, c), BLOCK, (l, name, c + 1)))
        for half in range(2):
            out.append(((l, "v", half), BLOCK, (l, "v", t_last)))
        for c in (0, 2):
            out.append(((l, "za", c), BLOCK, (l, "za", c + 1)))
        for n in range(2):
            for half in range(2):
                out.append(((l, "wo", n, half), BLOCK, (l, "wo", n, t_last)))
    for half in range(2):
        out.append(((2, "q", half), BLOCK, (2, "q", 3)))
    out.append(((2, "kv", 0), BLOCK, (2, "kv", 3)))
    for name in ("vin", "u", "gb"):
        for half in range(2):
            out.append(((2, name, half), BLOCK, (2, name, 3)))
    for c in (0, 2):
        out.append(((2, "ga", c), BLOCK, (2, "ga", c + 1)))
    for c in range(0, 16, 2):
        out.append(((2, "gm", c), BLOCK, (2, "gm", c + 1)))
    for n in range(2):
        for name in ("ya", "yb"):
            out.append(((2, name, 4 * n), BLOCK, (2, name, 4 * n + 3)))
    for n in range(2):
        for half in range(2):
            out.append(((2, "wo", n, half), BLOCK, (2, "wo", n, 3)))
    return out


BLOCKS = weight_blocks()
NUMBER = {key: n for n, (key, _, _) in enumerate(BLOCKS)}
AFTER = {}
for _n, (_, _, _last) in enumerate(BLOCKS):
    if _n + RING < len(BLOCKS):
        AFTER.setdefault(_last, []).append(_n + RING)

V_CONVW = 0
V_CONVB = V_CONVW + DEPTH * TAPS * CT
V_CLNG = V_CONVB + DEPTH * CT
V_CLNB = V_CLNG + DEPTH * CT
V_BMERGE = V_CLNB + DEPTH * CT
V_BSPAT = V_BMERGE + 2 * KD
V_COUNT = V_BSPAT + GROUPS


def y_slot(l, part, t):
    return (t + (part == "attn")) % 2


def output_after(l, t):
    tiles = list(query_tiles(l))
    return (tiles.index(t) + 1) * HEADS + 1 if t < 4 else None


def output2_after(t):
    return (t + 1) * HEADS + 1


class Signal:

    def __init__(self, sem, counted):
        self.sem = sem
        self.counted = counted
        self.steps = {}

    def mark(self, step):
        assert step not in self.steps, step
        self.steps[step] = len(self.steps) + 1
        return self.sem

    def at(self, step):
        if self.counted is None:
            return 1
        return self.counted[step]


def build(nc, io, counted):
    with ExitStack() as ctx:
        signals = {}
        known_bufs = counted["psum"] if counted else None
        psum_of = {}

        def signal(name):
            s = Signal(ctx.enter_context(nc.semaphore(name)), counted[name] if counted else None)
            signals[name] = s
            return s

        where = [1152]

        def sb(name, shape, dtype=F32, at=None):
            size = 2 if dtype == BF16 else 4
            n = size
            for s in shape[1:]:
                n *= s
            n = -(-n // 32) * 32
            offset = where[0] if at is None else at
            if at is None:
                where[0] += n
            return nc.alloc_sbuf_tensor_at(name, shape, dtype, offset=offset)

        whi = [sb(f"w_hi{i}", [P, BLOCK], F32R) for i in range(RING)]
        wlo = [sb(f"w_lo{i}", [P, BLOCK], F32R) for i in range(RING)]
        raw = [sb(f"w_raw{i}", [P, BLOCK]) for i in range(RAWS)]
        xhi = sb("x_hi", [P, KD, L], F32R)
        xlo = sb("x_lo", [P, KD, L], F32R)
        H_AT = where[0]
        h = sb("h", [P, 5, D])
        ident = sb("ident", [P, P])
        cos = sb("cos", [P, L])
        sin = sb("sin", [P, L])
        vec = sb("vec", [P, V_COUNT])
        wconv = sb("w_conv", [P, DEPTH * TAPS * CT])
        bmerge = sb("b_merge_half", [P, 2 * KD])
        widx = sb("w_idx", [P, 4, HEADS])
        stats = sb("stats", [P, 5, 2, 6])
        meanvar = sb("meanvar", [P, 5, 2])
        veps = sb("var_eps", [P, 16])
        rstd = sb("rstd", [P, 16])
        minus_half = sb("minus_half", [P, 16])
        top8 = sb("top8", [P, 4, 8])
        nmax = sb("neg_max", [P, 4])
        psums = sb("prob_sums", [P, 4])
        rsums = sb("prob_rsums", [P, 4])
        BLOCK2_AT = where[0]
        U_AT = where[0]
        u = sb("u", [P, CT, 560])
        acc = sb("conv_acc", [P, CT, L])
        zc = sb("zc", [P, CT, L])
        QI_AT = where[0]
        qi = sb("q_idx", [P, CT, L])
        za = sb("za", [P, CT, L], at=QI_AT)
        Q_AT = where[0]
        q = sb("q", [P, CT, L])
        relu = [sb(f"relu{i}", [P, L], at=Q_AT + 4 * L * i) for i in range(4)]
        K_AT = where[0]
        k = sb("k", [P, CT, L])
        xt0 = sb("x_first", [P, KD, L], at=Q_AT)
        ln_g = sb("post_ln_g", [P, D], at=Q_AT)
        ln_b = sb("post_ln_b", [P, D], at=Q_AT + 4 * D)
        gain = sb("norm_gain", [P, D], at=K_AT)
        hn = [sb(f"h_normed{i}", [P, D], at=Q_AT + 4 * D * 2 + 256 + 4 * D * (i + 1)) for i in range(1)]
        v = sb("v", [P, 5, DC])
        XS_AT = where[0]
        xs = [sb(f"shifted{i}", [P, L]) for i in range(4)]
        cnorm = [None] + [sb(f"conv_normed{t}", [P, DC], at=XS_AT + 2048 * (t - 1)) for t in MAIN]
        SC_AT = where[0]
        score = sb("score", [P, SCORES])
        pt = [sb(f"probs_t{i}", [P, 640], at=SC_AT + 2560 * i) for i in range(2)]
        ki = sb("k_idx", [P, L])
        mask = sb("mask", [P, SCORES + 16], BF16)
        wit = sb("w_idx_t", [P, L])
        e = [sb(f"exps{i}", [P, L]) for i in range(3)]
        yt = [sb(f"y_part{i}", [P, CT, P]) for i in range(2)]
        sl = [sb(f"conv_silu{i}", [P, CT, P]) for i in range(2)]
        cnorm[0] = sb("conv_normed0", [P, DC])
        assert where[0] <= nc.sbuf_usable_end, where[0]

        where[0] = BLOCK2_AT
        c2 = sb("axial_cos", [P, 4, HD])
        s2 = sb("axial_sin", [P, 4, HD])
        qg = sb("q_gain", [P, HD])
        kg = sb("k_gain", [P, HD])
        wst = sb("w_spatial_t", [P, GROUPS, P])
        lnv_g = sb("ln_v_g", [P, DC])
        lnv_b = sb("ln_v_b", [P, DC])
        gcq = sb("cos_gain_q", [P, 4, HD])
        gsq = sb("sin_gain_q", [P, 4, HD])
        gck = sb("cos_gain_k", [P, 4, HD])
        gsk = sb("sin_gain_k", [P, 4, HD])
        e2 = [sb(f"exps2_{i}", [P, SEQ], at=BLOCK2_AT + 2048 * i) for i in range(3)]
        pt2 = sb("probs2_t", [P, SEQ], at=BLOCK2_AT + 2048 * 3)
        yt2 = [sb(f"y2_part{i}", [P, SEQ], at=BLOCK2_AT + 2048 * (4 + i)) for i in range(2)]
        assert BLOCK2_AT + 2048 * 6 <= where[0]
        v2 = sb("v2", [P, 4, 2 * HD])
        ktd = sb("k2_t", [P, 2, SEQ])
        assert where[0] <= QI_AT
        where[0] = QI_AT
        qt = sb("q2_t", [P, CT, SEQ])
        sga = sb("silu_gate_a", [P, CT, SEQ])
        ug = sb("u_gated", [P, 4, DC])
        vv = sb("v_normed", [P, 4, DC])
        y2hi = sb("y2_hi", [P, KD, SEQ], F32R, at=QI_AT)
        y2lo = sb("y2_lo", [P, KD, SEQ], F32R, at=QI_AT + 4 * KD * SEQ)
        assert QI_AT + 8 * KD * SEQ <= where[0]
        TG_AT = where[0]
        tg = sb("merge_tanh", [P, 2 * KD, SEQ])
        gv = [sb(f"gelu_v{i}", [P, DC], at=TG_AT + 2048 * i) for i in range(2)]
        sgb = [sb(f"silu_gate_b{i}", [P, DC], at=TG_AT + 2048 * (2 + i)) for i in range(2)]
        qrow = [sb(f"qk_row{i}", [P, 10, HD], at=TG_AT + 8192 + 2560 * i) for i in range(2)]
        qrot = [sb(f"qk_rot{i}", [P, 10, HD], at=TG_AT + 8192 + 2560 * (2 + i)) for i in range(2)]
        qtmp = sb("qk_tmp", [P, 10, HD], at=TG_AT + 8192 + 2560 * 4)
        assert where[0] <= nc.sbuf_usable_end, where[0]
        fgain = sb("final_gain", [P, D], at=H_AT)

        bank = {x: ctx.enter_context(nc.psum_tensor(f"psum_{x}", [P, 2, 512], F32)) for x in "ABCD"}

        def psum(use):
            return bank[known_bufs[use] if known_bufs else "A"]

        raw_loaded = [ctx.enter_context(nc.semaphore(f"raw_loaded{i}")) for i in range(RAWS)]
        consts_loaded = ctx.enter_context(nc.semaphore("consts_loaded"))
        xt0_loaded = [ctx.enter_context(nc.semaphore(f"xt0_loaded{i}")) for i in range(4)]
        h_loaded = ctx.enter_context(nc.semaphore("h_loaded"))
        ln_loaded = ctx.enter_context(nc.semaphore("ln_loaded"))
        gain_loaded = ctx.enter_context(nc.semaphore("gain_loaded"))
        block2_loaded = ctx.enter_context(nc.semaphore("block2_loaded"))
        stored = ctx.enter_context(nc.semaphore("stored"))
        weights_hi = signal("weights_hi")
        weights_lo = signal("weights_lo")
        psum_full = signal("psum_full")
        act_took = signal("act_took")
        dve_took = signal("dve_took")
        hi_made = signal("hi_made")
        lo_made = signal("lo_made")
        exp_made = signal("exp_made")
        small_made = signal("small_made")
        u_made = signal("u_made")
        tap_done = signal("tap_done")
        rope_cos = signal("rope_cos")
        rope_sin = signal("rope_sin")
        rope_made = signal("rope_made")
        score_added = signal("score_added")
        causal_done = signal("causal_done")
        topk_max = signal("topk_max")
        topk_marked = signal("topk_marked")
        mask_made = signal("mask_made")
        rsum_made = signal("rsum_made")
        probs_made = signal("probs_made")
        y_made = signal("y_made")
        stats_made = signal("stats_made")
        dve_step = signal("dve_step")
        rstd_made = signal("rstd_made")
        pool_step = signal("pool_step")
        set_up = signal("set_up")
        normed = signal("normed")

        TAKEN_BY_DVE = {"fwd", "S", "wo", "xT", "vmix", "gmT", "ya", "yb"}

        def taken(use):
            if use[1] in ("O", "O2"):
                return y_made.sem, y_made.at((use[0], "attn", use[2]))
            by = dve_took if use[1] in TAKEN_BY_DVE else act_took
            return by.sem, by.at(use)

        items = {l: [(t, hd) for t in query_tiles(l) for hd in range(HEADS)] for l in range(DEPTH)}
        items2 = [(t, hd) for t in range(4) for hd in range(HEADS)]

        block = ctx.enter_context(nc.Block())

        @block.sync
        def _(sp):
            def load_weights(n):
                key, width, _ = BLOCKS[n]
                if n >= RAWS:
                    sp.wait_ge(weights_lo.sem, weights_lo.at(n - RAWS))
                sp.dma_start(raw[n % RAWS][:, 0:width], io["weights"][n, :, 0:width]) \
                    .then_inc(raw_loaded[n % RAWS], 16)

            def load_first_x(c):
                sp.dma_start(xt0[:, 2 * c:2 * c + 2, :], io["x_t"][:, 2 * c:2 * c + 2, :]) \
                    .then_inc(xt0_loaded[c], 16)

            def row(ap, n):
                return ap.rearrange("(o n) -> o n", o=1).broadcast_to([P, n])

            def load_post_ln(l):
                sp.wait_ge(psum_full.sem, psum_full.at((l, "O", 4)))
                sp.dma_start(ln_g[:, :], row(io["post_ln_g"][l], D)).then_inc(ln_loaded, 16)
                sp.dma_start(ln_b[:, :], row(io["post_ln_b"][l], D)).then_inc(ln_loaded, 16)
                if l == DEPTH - 1:
                    sp.dma_start(gain[:, :], row(io["norm_gain_2"][0], D)).then_inc(gain_loaded, 16)

            def load_block2():
                sp.wait_ge(psum_full.sem, psum_full.at((DEPTH - 1, "fwd", 4)))
                for dst, src in (
                    (c2[:, :, :], io["axial_cos"]), (s2[:, :, :], io["axial_sin"]),
                    (qg[:, :], row(io["q_gain_2"][0], HD)), (kg[:, :], row(io["k_gain_2"][0], HD)),
                    (wst[:, :, :], io["w_spatial_t"]),
                    (lnv_g[:, :], row(io["ln_v_gain_2"][0], DC)),
                    (lnv_b[:, :], row(io["ln_v_bias_2"][0], DC)),
                    (fgain[:, :], row(io["final_gain_2"], D)),
                ):
                    sp.dma_start(dst, src).then_inc(block2_loaded, 16)

            load_first_x(0)
            load_weights(0)
            for c in range(1, 4):
                load_first_x(c)
            load_weights(1)
            for dst, src in ((vec[:, :], io["vectors"]), (cos[:, :], io["rope_cos"]),
                             (sin[:, :], io["rope_sin"]), (ident[:, :], io["identity"])):
                sp.dma_start(dst, src).then_inc(consts_loaded, 16)
            sp.dma_start(h[0:META, 0, :], io["meta_tokens"]).then_inc(h_loaded, 16)
            sp.dma_start(h[:, 1:5, :], io["x"][0].rearrange("(t p) d -> p t d", p=P)).then_inc(h_loaded, 16)
            for n in range(2, len(BLOCKS)):
                key = BLOCKS[n][0]
                if key == (1, "a", 0):
                    load_post_ln(0)
                if key == (2, "q", 0):
                    load_block2()
                    load_post_ln(1)
                load_weights(n)
            for t in range(4):
                sp.wait_ge(normed.sem, normed.at(("out", t)))
                sp.dma_start(io["out"][0, P * t:P * t + P, :], h[:, t + 1, :]).then_inc(stored, 16)
            sp.wait_ge(stored, 64)

        @block.scalar
        def _(act):
            def split_hi(n):
                width = BLOCKS[n][1]
                act.wait_ge(raw_loaded[n % RAWS], 16 * (n // RAWS + 1))
                if n >= RING:
                    last = BLOCKS[n - RING][2]
                    act.wait_ge(psum_full.sem, psum_full.at(last))
                act.activation(whi[n % RING][:, 0:width], raw[n % RAWS][:, 0:width],
                               ACT.Copy).then_inc(weights_hi.mark(n), 1)

            def next_blocks(use):
                for n in AFTER.get(use, []):
                    split_hi(n)

            def full(use):
                act.wait_ge(psum_full.sem, psum_full.at(use))
                return psum(use)

            def halves(use, first):
                n = (L - first) // 2
                return full(use)[:, 0:2, 0:n], first

            def pair(ap):
                return ap.rearrange("p (a b) -> p a b", a=2)

            shift_uses = []

            def shift_buffer(step):
                n = len(shift_uses)
                if n >= 4:
                    sig, prev = shift_uses[n - 4]
                    act.wait_ge(sig.sem, sig.at(prev))
                return xs[n % 4]

            def take_channels(l, name, c):
                use = (l, name, c)
                first = META if l and name in ("zc", "za", "q", "qi") else 0
                ps, _ = halves(use, first)
                if name == "a":
                    if l == 1:
                        act.wait_ge(tap_done.sem, tap_done.at((0, c, TAPS - 1)))
                    act.activation(pair(u[:, c, PAD:PAD + L]), ps, ACT.Copy).then_inc(act_took.mark(use), 1)
                elif name == "g":
                    buf = shift_buffer(use)
                    act.activation(pair(buf[:, :]), ps, ACT.Tanh, scale=0.5).then_inc(act_took.mark(use), 1)
                    shift_uses.append((u_made, (l, c)))
                elif name == "zc" or name == "za":
                    dst = zc if name == "zc" else za
                    if name == "zc" and l == 1:
                        act.wait_ge(y_made.sem, y_made.at((0, "conv", 4)))
                    act.activation(pair(dst[:, c, first:L]), ps, ACT.Silu).then_inc(act_took.mark(use), 1)
                else:
                    dst = {"qi": qi, "q": q, "k": k}[name]
                    if name == "qi" and l == 1 and c == 0:
                        act.wait_ge(y_made.sem, y_made.at((0, "attn", 4)))
                    if name == "q" and c == 0:
                        act.wait_ge(score_added.sem, score_added.at((l, HEADS - 1, 4)))
                    buf = shift_buffer(use)
                    act.activation(pair(dst[:, c, first:L]), ps, ACT.Copy)
                    for s in range(4):
                        o = 32 * (s ^ 1)
                        got = act.activation(pair(buf[32 * s:32 * s + 32, first:L]), ps[o:o + 32], ACT.Copy)
                    got.then_inc(act_took.mark(use), 1)
                    shift_uses.append((rope_made, use))
                next_blocks(use)

            def take_index_keys(l):
                use = (l, "ki", 0)
                ps, _ = halves(use, 0)
                buf = shift_buffer(use)
                if l == 1:
                    act.wait_ge(psum_full.sem, psum_full.at((0, "idx", HEADS - 1, 4)))
                act.activation(pair(ki[0:HD, :]), ps[0:HD], ACT.Copy)
                act.activation(pair(wit[HD:HD + HEADS, :]), ps[HD:HD + HEADS], ACT.Copy)
                for s in range(2):
                    o = 32 * (s ^ 1)
                    got = act.activation(pair(buf[32 * s:32 * s + 32, :]), ps[o:o + 32], ACT.Copy)
                got.then_inc(act_took.mark(use), 1)
                shift_uses.append((rope_made, use))
                next_blocks(use)

            def index_weights(l):
                use = (l, "wT", 0)
                ps = full(use)
                act.activation(widx[:, :, :], ps[:, 0, 0:4 * HEADS].rearrange("p (t x) -> p t x", t=4),
                               ACT.Copy, scale=IDX_W_SCALE).then_inc(act_took.mark(use), 1)

            def index_relu(l):
                n = 0
                for hd in range(HEADS):
                    for t in MAIN:
                        use = (l, "idx", hd, t)
                        ps = full(use)
                        if n >= 4:
                            prev = n - 4
                            act.wait_ge(score_added.sem, score_added.at((l, prev // 4, prev % 4 + 1)))
                        if END[t] <= 512:
                            src, dst = ps[:, 0, 0:END[t]], relu[n % 4][:, 0:END[t]]
                        else:
                            src, dst = ps[:, 0:2, 0:END[t] // 2], pair(relu[n % 4][:, 0:END[t]])
                        act.activation(dst, src, ACT.Relu, scale=IDX_SCALE).then_inc(act_took.mark(use), 1)
                        n += 1

            def take_v(l, t):
                use = (l, "v", t)
                ps = full(use)
                act.activation(v[0:SIZE[t], t, :], ps[0:SIZE[t], 0, :], ACT.Copy).then_inc(act_took.mark(use), 1)
                next_blocks(use)

            def exps(l, i):
                t, hd = items[l][i]
                n = SIZE[t]
                act.wait_ge(dve_took.sem, dve_took.at((l, "S", t, hd)))
                act.activation(e[i % 3][0:n, 0:END[t]], e[i % 3][0:n, 0:END[t]], ACT.Exp, scale=-1.0,
                               bias=nmax[0:n, i % 4:i % 4 + 1],
                               accum_out=psums[0:n, i % 4:i % 4 + 1]).then_inc(exp_made.mark((l, i)), 1)

            def take_probs_t(l, i):
                t, hd = items[l][i]
                n = SIZE[t]
                use = (l, "PT", t, hd)
                ps = full(use)
                dst = pt[i % 2]
                if t:
                    act.activation(dst[:, 0:t * P], ps[:, 0, 0:t * P], ACT.Copy)
                act.activation(dst[0:META, SEQ:SEQ + n], ps[0:META, 1, 0:n], ACT.Copy).then_inc(act_took.mark(use), 1)

            def y_hi(l, part, t):
                c = 0 if part == "conv" else CT
                j = y_slot(l, part, t)
                act.wait_ge(y_made.sem, y_made.at((l, part, t)))
                act.activation(xhi[:, c:c + CT, START[t]:END[t]], yt[j][:, :, 0:SIZE[t]], ACT.Copy) \
                    .then_inc(hi_made.mark((l, part, t)), 1)

            def conv_silu(l, t):
                use = (l, "back", t)
                ps = full(use)
                prev = [s for s in query_tiles(l) if s < t - 1]
                if prev:
                    act.wait_ge(y_made.sem, y_made.at((l, "conv", t - 2)))
                n = SIZE[t]
                for c in range(CT):
                    got = act.activation(sl[t % 2][:, c, 0:n], ps[:, 0, c * P:c * P + n], ACT.Silu,
                                         scale=vec[:, V_CLNG + l * CT + c:V_CLNG + l * CT + c + 1],
                                         bias=vec[:, V_CLNB + l * CT + c:V_CLNB + l * CT + c + 1])
                got.then_inc(act_took.mark(use), 1)

            def x_hi(l, t):
                use = (l, "xT", t)
                ps = full(use)
                n = SIZE[t]
                act.activation(xhi[:, :, START[t]:END[t]],
                               ps[:, :, :].rearrange("p a (k n) -> p (a k) n", n=P)[:, :, 0:n], ACT.Copy) \
                    .then_inc(hi_made.mark((l, "x", t)), 1)

            for c in range(4):
                act.wait_ge(xt0_loaded[c], 16)
                act.activation(xhi[:, 2 * c:2 * c + 2, :], xt0[:, 2 * c:2 * c + 2, :], ACT.Copy) \
                    .then_inc(hi_made.mark((0, "x0", c)), 1)
                if c == 0:
                    split_hi(0)
            split_hi(1)
            split_hi(2)
            act.wait_ge(consts_loaded, 64)
            act.activation(wconv[:, :], vec[:, V_CONVW:V_CONVB], ACT.Copy, scale=0.5) \
                .then_inc(small_made.mark("wconv"), 1)
            act.activation(bmerge[:, :], vec[:, V_BMERGE:V_BSPAT], ACT.Copy, scale=0.5) \
                .then_inc(small_made.mark("bmerge"), 1)
            for l in range(DEPTH):
                for c in (0, 2):
                    for name in ("a", "g"):
                        take_channels(l, name, c)
                        take_channels(l, name, c + 1)
                for c in range(CT):
                    take_channels(l, "qi", c)
                take_index_keys(l)
                take_channels(l, "zc", 0)
                take_channels(l, "zc", 1)
                index_weights(l)
                index_relu(l)
                for name in ("q", "k"):
                    for c in range(CT):
                        take_channels(l, name, c)
                take_channels(l, "zc", 2)
                take_channels(l, "zc", 3)
                for t in TILES:
                    take_v(l, t)
                for c in range(CT):
                    take_channels(l, "za", c)
                n = len(items[l])
                exps(l, 0)
                for i in range(n):
                    if i + 1 < n:
                        exps(l, i + 1)
                    take_probs_t(l, i)
                    for t in query_tiles(l):
                        if i == output_after(l, t):
                            y_hi(l, "attn", t)
                for t in query_tiles(l):
                    conv_silu(l, t)
                    if t > query_tiles(l)[0]:
                        y_hi(l, "conv", t - 1)
                y_hi(l, "conv", 4)
                y_hi(l, "attn", 4)
                next_blocks((l, "wo", 0, 4))
                for t in query_tiles(l):
                    if t == 3:
                        next_blocks((l, "wo", 1, 4))
                    x_hi(l, t)

            def take_rows(name, t):
                use = (2, name, t)
                ps = full(use)
                if name == "q":
                    if t >= 2:
                        act.wait_ge(normed.sem, normed.at((2, "qk", t - 2)))
                    act.activation(qrow[t % 2][:, 0:8, :], ps[:, 0, :].rearrange("p (h d) -> p h d", d=HD), ACT.Copy) \
                        .then_inc(act_took.mark(use), 1)
                elif name == "kv":
                    act.activation(qrow[t % 2][:, 8:10, :], ps[:, 0, 0:P].rearrange("p (h d) -> p h d", d=HD), ACT.Copy)
                    act.activation(v2[:, t, :], ps[:, 0, P:2 * P], ACT.Copy).then_inc(act_took.mark(use), 1)
                elif name == "vin":
                    if t >= 2:
                        act.wait_ge(normed.sem, normed.at((2, "v", t - 2)))
                    act.activation(gv[t % 2][:, :], ps[:, 0, :], ACT.Gelu_apprx_tanh).then_inc(act_took.mark(use), 1)
                elif name == "u":
                    act.activation(ug[:, t, :], ps[:, 0, :], ACT.Gelu_apprx_tanh).then_inc(act_took.mark(use), 1)
                else:
                    if t >= 2:
                        act.wait_ge(normed.sem, normed.at((2, "ug", t - 2)))
                    act.activation(sgb[t % 2][:, :], ps[:, 0, :], ACT.Silu).then_inc(act_took.mark(use), 1)
                next_blocks(use)

            def take_gates(name, c):
                use = (2, name, c)
                ps = full(use)
                if name == "ga":
                    act.activation(sga[:, c, :], ps[:, 0, :], ACT.Silu).then_inc(act_took.mark(use), 1)
                else:
                    if c == 0:
                        act.wait_ge(normed.sem, normed.at((2, "ug", 3)))
                    act.activation(tg[:, c, :], ps[:, 0, :], ACT.Tanh, scale=0.5, bias=bmerge[:, c:c + 1]) \
                        .then_inc(act_took.mark(use), 1)
                next_blocks(use)

            def take_qk_t(t):
                use = (2, "qkT", t)
                ps = full(use)
                c0, c1 = P * t, P * t + P
                act.activation(qt[:, :, c0:c1], ps[:, 0, :].rearrange("p (c n) -> p c n", n=P), ACT.Copy)
                for g in range(2):
                    for s in range(2):
                        got = act.activation(ktd[HD * s:HD * s + HD, g, c0:c1],
                                             ps[HD * g:HD * g + HD, 1, 0:P], ACT.Copy)
                got.then_inc(act_took.mark(use), 1)

            def exps2(i):
                t, hd = items2[i]
                use = (2, "S2", t, hd)
                act.wait_ge(rsum_made.sem, rsum_made.at((2, "max", i)))
                act.activation(e2[i % 3][:, :], psum(use)[:, 0, :], ACT.Exp, bias=nmax[:, i % 4:i % 4 + 1],
                               accum_out=psums[:, i % 4:i % 4 + 1]).then_inc(act_took.mark(use), 1)

            def take_probs2_t(i):
                t, hd = items2[i]
                use = (2, "PT2", t, hd)
                ps = full(use)
                if i:
                    pt_, ph = items2[i - 1]
                    act.wait_ge(psum_full.sem, psum_full.at((2, "PV2", pt_, ph)))
                act.activation(pt2[:, :], ps[:, 0, :], ACT.Copy).then_inc(act_took.mark(use), 1)

            def part_hi(part, t):
                c0, c1 = P * t, P * t + P
                if part == "gm":
                    ps = full((2, "gmT", t))
                    act.activation(xhi[:, CT:2 * CT, c0:c1], ps[:, 0, :].rearrange("p (c n) -> p c n", n=P), ACT.Copy) \
                        .then_inc(hi_made.mark((2, "gm", t)), 1)
                else:
                    act.wait_ge(y_made.sem, y_made.at((2, "attn", t)))
                    act.activation(xhi[:, 0:CT, c0:c1], yt2[t % 2][:, :].rearrange("p (c n) -> p c n", n=P), ACT.Copy) \
                        .then_inc(hi_made.mark((2, "attn", t)), 1)

            def y2_hi(d):
                act.wait_ge(y_made.sem, y_made.at((2, "y", d)))
                act.activation(y2hi[:, d, :], yt2[d % 2][:, :], ACT.Copy).then_inc(hi_made.mark((2, "y", d)), 1)

            for t in range(4):
                take_rows("q", t)
                take_rows("kv", t)
            for name in ("vin", "u", "gb"):
                for t in range(4):
                    take_rows(name, t)
                    if name == "vin":
                        take_qk_t(t)
            for c in range(CT):
                take_gates("ga", c)
            for c in range(2 * KD):
                take_gates("gm", c)
            for t in range(4):
                part_hi("gm", t)
            n = len(items2)
            exps2(0)
            for i in range(n):
                if i + 1 < n:
                    exps2(i + 1)
                take_probs2_t(i)
                for t in range(3):
                    if i == output2_after(t):
                        part_hi("attn", t)
            part_hi("attn", 3)
            for d in range(KD):
                if d == 4:
                    next_blocks((2, "ya", 3))
                    next_blocks((2, "yb", 3))
                y2_hi(d)
            next_blocks((2, "ya", 7))
            next_blocks((2, "yb", 7))
            next_blocks((2, "wo", 0, 3))
            for t in range(4):
                act.wait_ge(dve_took.sem, dve_took.at((2, "wo", 1, t)))
                act.activation(tg[:, 2 * t:2 * t + 2, :], h[:, t + 1, :].rearrange("p (a b) -> p a b", a=2), ACT.Square,
                               accum_out=psums[:, t:t + 1]).then_inc(exp_made.mark(("out", t)), 1)

        @block.gpsimd
        def _(pool):
            def split_lo(n):
                width = BLOCKS[n][1]
                pool.wait_ge(weights_hi.sem, weights_hi.at(n))
                cut = [0, width // 2, width]
                for a, b in zip(cut, cut[1:]):
                    got = pool.tensor_tensor(wlo[n % RING][:, a:b], raw[n % RAWS][:, a:b],
                                             whi[n % RING][:, a:b].bitcast(F32), ALU.subtract)
                got.then_inc(weights_lo.mark(n), 1)

            def next_blocks(use):
                for n in AFTER.get(use, []):
                    split_lo(n)

            shifts = [0]

            def times_sin(l, name, c):
                use = (l, name, c)
                first = META if l and name in ("q", "qi") else 0
                rows = HD if name == "ki" else P
                buf = xs[shifts[0] % 4]
                shifts[0] += 1
                pool.wait_ge(act_took.sem, act_took.at(use))
                pool.tensor_tensor(buf[0:rows, first:L], buf[0:rows, first:L], sin[0:rows, first:L], ALU.mult) \
                    .then_inc(rope_sin.mark(use), 1)

            def reciprocal_deviation(step, src, n, rows, slot, scale, eps):
                pool.tensor_scalar(veps[0:rows, slot:slot + n], src, scale, eps, ALU.mult, ALU.add) \
                    .then_inc(pool_step.mark(step), 1)
                pool.wait_ge(pool_step.sem, pool_step.at(step))
                pool.tensor_tensor(rstd[0:rows, slot:slot + n], veps[0:rows, slot:slot + n],
                                   minus_half[0:rows, 0:n], ALU.pow).then_inc(rstd_made.mark(step), 1)

            def ln_deviation(step, t, rows):
                pool.wait_ge(stats_made.sem, stats_made.at(step))
                reciprocal_deviation(step, meanvar[0:rows, t, 1:2], 1, rows, t, 1.0, LN_EPS)

            pool.memset(u[:, :, 0:PAD], 0.0).then_inc(set_up.mark("pad"), 1)
            pool.memset(minus_half[:, :], -0.5).then_inc(set_up.mark("half"), 1)
            pool.memset(mask[0:META, MASK0_AT:MASK0_AT + META], 0.0).then_inc(set_up.mark("mask"), 1)
            pool.wait_ge(set_up.sem, set_up.at("mask"))
            pool.affine_select(out=mask[0:META, MASK0_AT:MASK0_AT + META],
                               in_=mask[0:META, MASK0_AT:MASK0_AT + META], compare_op=ALU.is_ge, fill=HIDE,
                               base=0, pattern=[[-1, META]], channel_multiplier=1) \
                .then_inc(set_up.mark("mask0"), 1)
            for n in range(RING):
                split_lo(n)
            pool.wait_ge(consts_loaded, 64)
            for l in range(DEPTH):
                for c in (0, 2):
                    for name in ("a", "g"):
                        next_blocks((l, name, c + 1))
                for c in range(CT):
                    if c == 0:
                        shifts[0] += 4
                    times_sin(l, "qi", c)
                    next_blocks((l, "qi", c))
                times_sin(l, "ki", 0)
                next_blocks((l, "ki", 0))
                next_blocks((l, "zc", 1))
                for t in MAIN:
                    a = SCORE_AT[t] + START[t]
                    pool.wait_ge(score_added.sem, score_added.at((l, HEADS - 1, t)))
                    pool.affine_select(out=score[:, a:a + P], in_=score[:, a:a + P], compare_op=ALU.is_ge,
                                       fill=FILL, base=0, pattern=[[-1, P]], channel_multiplier=1) \
                        .then_inc(causal_done.mark((l, "score", t)), 1)
                for name in ("q", "k"):
                    for c in range(CT):
                        times_sin(l, name, c)
                        next_blocks((l, name, c))
                next_blocks((l, "zc", 3))
                next_blocks((l, "v", 4))
                for t in MAIN:
                    a = SCORE_AT[t] + START[t]
                    pool.wait_ge(mask_made.sem, mask_made.at((l, t)))
                    pool.affine_select(out=mask[:, a:a + P], in_=mask[:, a:a + P], compare_op=ALU.is_ge,
                                       fill=HIDE, base=0, pattern=[[-1, P]], channel_multiplier=1) \
                        .then_inc(causal_done.mark((l, "mask", t)), 1)
                for t in query_tiles(l):
                    ln_deviation((l, "conv", t), t, SIZE[t])
                next_blocks((l, "za", 1))
                next_blocks((l, "za", 3))
                next_blocks((l, "wo", 0, 4))
                for t in query_tiles(l):
                    if t == 3:
                        next_blocks((l, "wo", 1, 4))
                    ln_deviation((l, "post", t), t, SIZE[t])
                    if l == DEPTH - 1:
                        pool.wait_ge(stats_made.sem, stats_made.at((2, "in", t)))
                        reciprocal_deviation((2, "in", t), psums[:, t - 1:t], 1, P, 8 + t, 1.0 / D, EPS)
            for t in range(4):
                if t == 3:
                    next_blocks((2, "q", 3))
                    next_blocks((2, "kv", 3))
                pool.wait_ge(stats_made.sem, stats_made.at((2, "qk", t)))
                reciprocal_deviation((2, "qk", t), veps[:, 0:10], 10, P, 0, 1.0 / HD, EPS)
            for name in ("vin", "u", "gb"):
                if name == "vin":
                    for t in range(4):
                        if t == 3:
                            next_blocks((2, name, 3))
                        pool.wait_ge(stats_made.sem, stats_made.at((2, "v", t)))
                        reciprocal_deviation((2, "v", t), meanvar[:, t, 1:2], 1, P, 12 + t, 1.0, EPS)
                else:
                    next_blocks((2, name, 3))
            for c in (1, 3):
                next_blocks((2, "ga", c))
            for c in range(1, 2 * KD, 2):
                next_blocks((2, "gm", c))
            for d in (3, 7):
                next_blocks((2, "ya", d))
                next_blocks((2, "yb", d))
            next_blocks((2, "wo", 0, 3))
            for t in range(4):
                pool.wait_ge(exp_made.sem, exp_made.at(("out", t)))
                reciprocal_deviation(("out", t), psums[:, t:t + 1], 1, P, t, 1.0 / D, EPS)

        @block.tensor
        def _(pe):
            last_use = {}
            turn = {"AB": 0, "CD": 0}

            def claim(use, buf):
                if buf in last_use:
                    prev = last_use[buf]
                    pe.wait_ge(*taken(prev))
                last_use[buf] = use
                psum_of[use] = buf
                return bank[buf]

            def next_buf(kind):
                turn[kind] += 1
                return kind[turn[kind] % 2]

            def weights(n):
                pe.wait_ge(weights_lo.sem, weights_lo.at(n))
                return whi[n % RING], wlo[n % RING]

            x = (xhi, xlo)

            def channels(l, name, c, waits=None):
                use = (l, name, c)
                if name == "ki":
                    n, width, cols, at = NUMBER[use], HD + HEADS, HD + HEADS, 0
                else:
                    n, width, cols, at = NUMBER[(l, name, c - c % 2)], 2 * P, P, c % 2 * P
                w = [part[:, 0:KD * width].rearrange("p (k c) -> p k c", k=KD) for part in weights(n)]
                if l == 2:
                    pieces = ((META, L),)
                else:
                    pieces = column_halves(META if l and name in ("zc", "za", "q", "qi") else 0)
                ps = claim(use, next_buf("AB"))
                for kt in range(KD):
                    if waits:
                        waits(kt)
                    for wp, xp in PASSES:
                        for i, (a, b) in enumerate(pieces):
                            mm = pe.matmul(ps[0:cols, i, 0:b - a], w[wp][:, kt, at:at + cols], x[xp][:, kt, a:b],
                                           start=(kt == 0 and wp + xp == 0), stop=(kt == KD - 1 and wp == 1))
                mm.then_inc(psum_full.mark(use), 1)

            def rows(use, first_block, act_parts, c0, n_blocks, width=DC, at=0, kts=4):
                ps = claim(use, next_buf("AB"))
                for half in range(n_blocks):
                    w = [part[:, :].rearrange("p (k c) -> p k c", k=kts) for part in weights(first_block + half)]
                    for kk in range(kts):
                        kt = half * kts + kk
                        for wp, xp in PASSES:
                            mm = pe.matmul(ps[:, 0, 0:width], act_parts[xp][:, kt, c0:c0 + P], w[wp][:, kk, at:at + width],
                                           start=(kt == 0 and wp + xp == 0), stop=(kt == KD - 1 and wp == 1))
                mm.then_inc(psum_full.mark(use), 1)

            def index_weights(l):
                use = (l, "wT", 0)
                ps = claim(use, next_buf("CD"))
                pe.wait_ge(act_took.sem, act_took.at((l, "ki", 0)))
                for t in MAIN:
                    mm = pe.transpose(ps[:, 0, (t - 1) * HEADS:t * HEADS], wit[HD:HD + HEADS, START[t]:END[t]],
                                      ident[HD:HD + HEADS, HD:HD + HEADS])
                mm.then_inc(psum_full.mark(use), 1)

            def logits(use, ps, qs, ks, hd, t, n_keys):
                s = HD * (hd % 2)
                lhs = qs[s:s + HD, hd // 2, START[t]:END[t]]
                if n_keys <= 512:
                    pieces = ((0, n_keys),)
                else:
                    pieces = ((0, n_keys // 2), (n_keys // 2, n_keys))
                for i, (a, b) in enumerate(pieces):
                    mm = pe.matmul(ps[0:SIZE[t], i, 0:b - a], lhs, ks[s:s + HD, a:b], start=True, stop=True)
                mm.then_inc(psum_full.mark(use), 1)

            def index_scores(l):
                pe.wait_ge(rope_made.sem, rope_made.at((l, "ki", "copy")))
                for hd in range(HEADS):
                    for t in MAIN:
                        use = (l, "idx", hd, t)
                        logits(use, claim(use, next_buf("CD")), qi, ki, hd, t, END[t])

            def attention_logits(l, i):
                t, hd = items[l][i]
                use = (l, "S", t, hd)
                logits(use, claim(use, next_buf("CD")), q, k[:, hd // 2, :], hd, t, END[t])

            def turn_probs(l, i):
                t, hd = items[l][i]
                n = SIZE[t]
                use = (l, "PT", t, hd)
                ps = claim(use, "A")
                pe.wait_ge(probs_made.sem, probs_made.at((l, i)))
                src = e[i % 3]
                for j in range(1, t + 1):
                    pe.transpose(ps[:, 0, (j - 1) * P:(j - 1) * P + n], src[0:n, START[j]:END[j]], ident[0:n, 0:n])
                pe.transpose(ps[0:META, 1, 0:n], src[0:n, 0:META], ident[0:n, 0:n]) \
                    .then_inc(psum_full.mark(use), 1)

            def probs_times_v(l, i):
                t, hd = items[l][i]
                n = SIZE[t]
                use = (l, "O", t)
                ps = claim(use, "B") if hd == 0 else bank["B"]
                pe.wait_ge(act_took.sem, act_took.at((l, "PT", t, hd)))
                s = HD * (hd % 2)
                out = ps[s:s + HD, 0, hd // 2 * P:hd // 2 * P + n]
                src = pt[i % 2]
                mm = pe.matmul(out, v[0:META, 0, hd * HD:hd * HD + HD], src[0:META, SEQ:SEQ + n],
                               start=True, stop=(t == 0))
                for j in range(1, t + 1):
                    mm = pe.matmul(out, v[:, j, hd * HD:hd * HD + HD], src[:, (j - 1) * P:(j - 1) * P + n],
                                   start=False, stop=(j == t))
                if hd == HEADS - 1:
                    mm.then_inc(psum_full.mark(use), 1)

            def turn_conv(l, t):
                use = (l, "fwd", t)
                ps = claim(use, next_buf("AB"))
                n = SIZE[t]
                for c in range(CT):
                    pe.wait_ge(tap_done.sem, tap_done.at((l, c, TAPS - 1)))
                    mm = pe.transpose(ps[0:n, 0, c * P:c * P + P], acc[:, c, START[t]:END[t]], ident[:, :])
                mm.then_inc(psum_full.mark(use), 1)

            def turn_conv_back(l, t):
                use = (l, "back", t)
                ps = claim(use, next_buf("CD"))
                n = SIZE[t]
                pe.wait_ge(dve_took.sem, dve_took.at((l, "fwd", t)))
                for c in range(CT):
                    mm = pe.transpose(ps[:, 0, c * P:c * P + n], cnorm[t][0:n, c * P:c * P + P], ident[0:n, 0:n])
                mm.then_inc(psum_full.mark(use), 1)

            def turn_rows(l, t):
                use = (l, "xT", t)
                ps = claim(use, next_buf("CD"))
                n = SIZE[t]
                pe.wait_ge(normed.sem, normed.at((l, "x", t)))
                src = h[0:n, t, :] if l == 0 else hn[0][0:n, :]
                for kt in range(KD):
                    mm = pe.transpose(ps[:, kt // 4, kt % 4 * P:kt % 4 * P + n], src[:, kt * P:kt * P + P], ident[0:n, 0:n])
                mm.then_inc(psum_full.mark(use), 1)

            for l in range(DEPTH):
                if l == 0:
                    def first_x(kt):
                        if kt % 2 == 0:
                            pe.wait_ge(lo_made.sem, lo_made.at((0, "x0", kt // 2)))
                else:
                    first_x = None
                    for t in TILES:
                        pe.wait_ge(dve_took.sem, dve_took.at((l - 1, "xT", t)))
                for c in (0, 2):
                    for name in ("a", "g"):
                        for cc in (c, c + 1):
                            channels(l, name, cc, first_x)
                            first_x = None
                for c in range(CT):
                    channels(l, "qi", c)
                channels(l, "ki", 0)
                channels(l, "zc", 0)
                channels(l, "zc", 1)
                index_weights(l)
                for c in range(CT):
                    pe.wait_ge(rope_made.sem, rope_made.at((l, "qi", c)))
                index_scores(l)
                for name in ("q", "k"):
                    for c in range(CT):
                        channels(l, name, c)
                channels(l, "zc", 2)
                channels(l, "zc", 3)
                for t in TILES:
                    rows((l, "v", t), NUMBER[(l, "v", 0)], x, START[t], 2)
                for c in range(CT):
                    channels(l, "za", c)
                for t in query_tiles(l):
                    turn_conv(l, t)
                n = len(items[l])
                for c in range(CT):
                    pe.wait_ge(rope_made.sem, rope_made.at((l, "q", c)))
                    pe.wait_ge(rope_made.sem, rope_made.at((l, "k", c)))
                attention_logits(l, 0)
                attention_logits(l, 1)
                for i in range(n):
                    if i + 2 < n:
                        attention_logits(l, i + 2)
                    turn_probs(l, i)
                    if i:
                        probs_times_v(l, i - 1)
                probs_times_v(l, n - 1)
                for t in query_tiles(l):
                    turn_conv_back(l, t)
                for t in query_tiles(l):
                    pe.wait_ge(lo_made.sem, lo_made.at((l, "conv", t)))
                    pe.wait_ge(lo_made.sem, lo_made.at((l, "attn", t)))
                for half in range(2):
                    for t in query_tiles(l):
                        rows((l, "wo", half, t), NUMBER[(l, "wo", half, 0)], x, START[t], 2)
                        if half == 1 and t > query_tiles(l)[0] + 1:
                            turn_rows(l, t - 2)
                turn_rows(l, 3)
                turn_rows(l, 4)

            def turn_qk(t):
                use = (2, "qkT", t)
                ps = claim(use, next_buf("CD"))
                pe.wait_ge(normed.sem, normed.at((2, "rope", t)))
                src = qrot[t % 2][:, :, :].rearrange("p h d -> p (h d)")
                for c in range(5):
                    mm = pe.transpose(ps[:, c // 4, c % 4 * P:c % 4 * P + P], src[:, c * P:c * P + P], ident[:, :])
                mm.then_inc(psum_full.mark(use), 1)

            def mix_positions(pair_):
                use = (2, "vmix", pair_)
                ps = claim(use, next_buf("CD"))
                for t in range(4):
                    pe.wait_ge(normed.sem, normed.at((2, "v", t)))
                pe.wait_ge(block2_loaded, 8 * 16)
                for i in range(2):
                    g = 2 * pair_ + i
                    mm = pe.matmul(ps[:, i, 0:4 * GD], wst[:, g, :], vv[:, :, g * GD:g * GD + GD], start=True, stop=True)
                mm.then_inc(psum_full.mark(use), 1)

            def turn_mlp(t):
                use = (2, "gmT", t)
                ps = claim(use, next_buf("CD"))
                for pair_ in range(4):
                    pe.wait_ge(dve_took.sem, dve_took.at((2, "vmix", pair_)))
                for c in range(CT):
                    mm = pe.transpose(ps[:, 0, c * P:c * P + P], ug[:, t, c * P:c * P + P], ident[:, :])
                mm.then_inc(psum_full.mark(use), 1)

            def logits2(i):
                t, hd = items2[i]
                use = (2, "S2", t, hd)
                ps = claim(use, next_buf("CD"))
                s = HD * (hd % 2)
                pe.matmul(ps[:, 0, :], qt[s:s + HD, hd // 2, P * t:P * t + P], ktd[s:s + HD, hd // 4, :],
                          start=True, stop=True).then_inc(psum_full.mark(use), 1)

            def turn_probs2(i):
                t, hd = items2[i]
                use = (2, "PT2", t, hd)
                ps = claim(use, "A")
                pe.wait_ge(probs_made.sem, probs_made.at((2, i)))
                for j in range(4):
                    mm = pe.transpose(ps[:, 0, j * P:j * P + P], e2[i % 3][:, j * P:j * P + P], ident[:, :])
                mm.then_inc(psum_full.mark(use), 1)

            def probs_times_v2(i):
                t, hd = items2[i]
                ps = claim((2, "O2", t), "B") if hd == 0 else bank["B"]
                pe.wait_ge(act_took.sem, act_took.at((2, "PT2", t, hd)))
                s, g = HD * (hd % 2), hd // 4
                for j in range(4):
                    mm = pe.matmul(ps[s:s + HD, 0, hd // 2 * P:hd // 2 * P + P], v2[:, j, g * HD:g * HD + HD],
                                   pt2[:, j * P:j * P + P], start=(j == 0), stop=(j == 3))
                mm.then_inc(psum_full.mark((2, "PV2", t, hd)), 1)

            def branch(name, d):
                use = (2, name, d)
                n = NUMBER[(2, name, d - d % 4)]
                w = [part[:, :].rearrange("p (k c) -> p k c", k=CT) for part in weights(n)]
                k0 = 0 if name == "ya" else CT
                ps = claim(use, next_buf("AB"))
                for kt in range(CT):
                    for wp, xp in PASSES:
                        mm = pe.matmul(ps[:, 0, :], w[wp][:, kt, d % 4 * P:d % 4 * P + P], x[xp][:, k0 + kt, 0:SEQ],
                                       start=(kt == 0 and wp + xp == 0), stop=(kt == CT - 1 and wp == 1))
                mm.then_inc(psum_full.mark(use), 1)

            for t in MAIN:
                pe.wait_ge(dve_took.sem, dve_took.at((1, "xT", t)))
            for t in range(4):
                rows((2, "q", t), NUMBER[(2, "q", 0)], x, META + P * t, 2)
                rows((2, "kv", t), NUMBER[(2, "kv", 0)], x, META + P * t, 1, 2 * P, 0, KD)
            for name in ("vin", "u", "gb"):
                for t in range(4):
                    rows((2, name, t), NUMBER[(2, name, 0)], x, META + P * t, 2)
                    if name == "vin":
                        turn_qk(t)
            for c in range(CT):
                channels(2, "ga", c)
            for c in range(2 * KD):
                channels(2, "gm", c)
            for pair_ in range(4):
                mix_positions(pair_)
            for t in range(4):
                turn_mlp(t)
            n = len(items2)
            logits2(0)
            logits2(1)
            for i in range(n):
                if i + 2 < n:
                    logits2(i + 2)
                turn_probs2(i)
                if i:
                    probs_times_v2(i - 1)
            probs_times_v2(n - 1)
            for t in range(4):
                pe.wait_ge(lo_made.sem, lo_made.at((2, "attn", t)))
                pe.wait_ge(dve_took.sem, dve_took.at((2, "gmT", t)))
            for half in range(2):
                for d in range(4 * half, 4 * half + 4):
                    branch("ya", d)
                    branch("yb", d)
            for d in range(KD):
                pe.wait_ge(lo_made.sem, lo_made.at((2, "y", d)))
            for half in range(2):
                for t in range(4):
                    rows((2, "wo", half, t), NUMBER[(2, "wo", half, 0)], (y2hi, y2lo), P * t, 2)

        @block.vector
        def _(dve):
            def full(use):
                dve.wait_ge(psum_full.sem, psum_full.at(use))
                return psum(use)

            def pair(ap):
                return ap.rearrange("p (a b) -> p a b", a=2)

            shifts = [0]

            def gate_conv_input(l, c):
                buf = xs[shifts[0] % 4]
                shifts[0] += 1
                dve.wait_ge(act_took.sem, act_took.at((l, "g", c)))
                dve.scalar_tensor_tensor(u[:, c, PAD:PAD + L], buf[:, :], 1.0, u[:, c, PAD:PAD + L],
                                         ALU.add, ALU.mult).then_inc(u_made.mark((l, c)), 1)

            def conv(l, c, first, last):
                x0 = META if l else 0
                for tap in range(first, last):
                    for cc in (c, c + 1):
                        w = wconv[:, (l * TAPS + tap) * CT + cc:(l * TAPS + tap) * CT + cc + 1]
                        src = u[:, cc, tap + x0:tap + L]
                        dst = acc[:, cc, x0:L]
                        if tap == 0:
                            dve.wait_ge(u_made.sem, u_made.at((l, cc)))
                            b = vec[:, V_CONVB + l * CT + cc:V_CONVB + l * CT + cc + 1]
                            got = dve.tensor_scalar(dst, src, w, b, ALU.mult, ALU.add)
                        else:
                            dve.wait_ge(tap_done.sem, tap_done.at((l, cc, tap - 1)))
                            got = dve.scalar_tensor_tensor(dst, src, w, dst, ALU.mult, ALU.add)
                        got.then_inc(tap_done.mark((l, cc, tap)), 1)

            def rope(l, name, c):
                use = (l, name, c)
                first = META if l and name in ("q", "qi") else 0
                n = HD if name == "ki" else P
                buf = xs[shifts[0] % 4]
                shifts[0] += 1
                dst = ki[0:n, :] if name == "ki" else {"qi": qi, "q": q, "k": k}[name][:, c, first:L]
                dve.wait_ge(act_took.sem, act_took.at(use))
                dve.tensor_tensor(dst, dst, cos[0:n, first:L], ALU.mult).then_inc(rope_cos.mark(use), 1)
                dve.wait_ge(rope_cos.sem, rope_cos.at(use))
                dve.wait_ge(rope_sin.sem, rope_sin.at(use))
                dve.tensor_tensor(dst, dst, buf[0:n, first:L], ALU.add).then_inc(rope_made.mark(use), 1)
                if name == "ki":
                    dve.wait_ge(rope_made.sem, rope_made.at(use))
                    dve.tensor_copy(ki[HD:P, :], ki[0:HD, :]).then_inc(rope_made.mark((l, "ki", "copy")), 1)

            def add_scores(l):
                n = 0
                dve.wait_ge(act_took.sem, act_took.at((l, "wT", 0)))
                for hd in range(HEADS):
                    for t in MAIN:
                        dve.wait_ge(act_took.sem, act_took.at((l, "idx", hd, t)))
                        dst = score[:, SCORE_AT[t]:SCORE_AT[t] + END[t]]
                        src = relu[n % 4][:, 0:END[t]]
                        w = widx[:, t - 1, hd:hd + 1]
                        if hd == 0:
                            got = dve.tensor_scalar(dst, src, w, 0.0, ALU.mult, ALU.add)
                        else:
                            dve.wait_ge(score_added.sem, score_added.at((l, hd - 1, t)))
                            got = dve.scalar_tensor_tensor(dst, src, w, dst, ALU.mult, ALU.add)
                        got.then_inc(score_added.mark((l, hd, t)), 1)
                        n += 1

            def topk(l, between):
                rounds = -(-TOPK // 8)
                for r in range(rounds):
                    for t in MAIN:
                        vals = score[:, SCORE_AT[t]:SCORE_AT[t] + END[t]]
                        if r == 0:
                            dve.wait_ge(causal_done.sem, causal_done.at((l, "score", t)))
                        else:
                            dve.wait_ge(topk_marked.sem, topk_marked.at((l, r - 1, t)))
                        dve.max(top8[:, t - 1, :], vals).then_inc(topk_max.mark((l, r, t)), 1)
                    if r == rounds - 1:
                        dve.wait_ge(topk_max.sem, topk_max.at((l, r, 4)))
                        dve.memset(top8[:, :, TOPK - 8 * r:8], MARK).then_inc(topk_max.mark((l, "cut")), 1)
                        dve.wait_ge(topk_max.sem, topk_max.at((l, "cut")))
                    for t in MAIN:
                        vals = score[:, SCORE_AT[t]:SCORE_AT[t] + END[t]]
                        dve.wait_ge(topk_max.sem, topk_max.at((l, r, t)))
                        dve.match_replace(vals, top8[:, t - 1, :], vals, MARK).then_inc(topk_marked.mark((l, r, t)), 1)
                    between(r)
                for t in MAIN:
                    a, b = SCORE_AT[t], SCORE_AT[t] + END[t]
                    dve.wait_ge(topk_marked.sem, topk_marked.at((l, rounds - 1, t)))
                    dve.tensor_scalar(mask[:, a:b], score[:, a:b], MARK, HIDE, ALU.not_equal, ALU.mult) \
                        .then_inc(mask_made.mark((l, t)), 1)

            def conv_stats(l, t):
                ps = full((l, "fwd", t))
                n = SIZE[t]
                step = (l, "conv", t)
                dve.bn_stats(stats[0:n, t, 0, :], ps[0:n, 0, :]).then_inc(dve_step.mark(step), 1)
                dve.wait_ge(dve_step.sem, dve_step.at(step))
                dve.bn_aggr(meanvar[0:n, t, :], stats[0:n, t, 0, :]).then_inc(stats_made.mark(step), 1)

            def conv_norm(l, t):
                use = (l, "fwd", t)
                n = SIZE[t]
                dve.wait_ge(stats_made.sem, stats_made.at((l, "conv", t)))
                dve.wait_ge(rstd_made.sem, rstd_made.at((l, "conv", t)))
                dve.tensor_scalar(cnorm[t][0:n, :], psum(use)[0:n, 0, :], meanvar[0:n, t, 0:1], rstd[0:n, t:t + 1],
                                  ALU.subtract, ALU.mult).then_inc(dve_took.mark(use), 1)

            def masked_logits(l, i):
                t, hd = items[l][i]
                n = SIZE[t]
                use = (l, "S", t, hd)
                ps = full(use)
                if hd == 0 and t:
                    dve.wait_ge(causal_done.sem, causal_done.at((l, "mask", t)))
                if i >= 3:
                    dve.wait_ge(psum_full.sem, psum_full.at((l, "PT", *items[l][i - 3])))
                a = SCORE_AT[t] if t else MASK0_AT
                m = mask[0:n, a:a + END[t]]
                dst = e[i % 3][0:n, 0:END[t]]
                if END[t] <= 512:
                    src = ps[0:n, 0, 0:END[t]]
                else:
                    src, m, dst = ps[0:n, 0:2, 0:END[t] // 2], pair(m), pair(dst)
                dve.tensor_tensor_reduce(dst, src, m, -SCALE, 3.0e38, ALU.add, ALU.min,
                                         nmax[0:n, i % 4:i % 4 + 1]).then_inc(dve_took.mark(use), 1)

            def normalise(l, i):
                t, hd = items[l][i]
                n = SIZE[t]
                dve.wait_ge(exp_made.sem, exp_made.at((l, i)))
                dve.reciprocal(rsums[0:n, i % 4:i % 4 + 1], psums[0:n, i % 4:i % 4 + 1]).then_inc(rsum_made.mark((l, i)), 1)
                dve.wait_ge(rsum_made.sem, rsum_made.at((l, i)))
                dve.tensor_scalar(e[i % 3][0:n, 0:END[t]], e[i % 3][0:n, 0:END[t]], rsums[0:n, i % 4:i % 4 + 1], None,
                                  ALU.mult).then_inc(probs_made.mark((l, i)), 1)

            y_parts = {}

            def y_part(l, part, t):
                n = SIZE[t]
                j = y_slot(l, part, t)
                if j in y_parts:
                    dve.wait_ge(lo_made.sem, lo_made.at(y_parts[j]))
                y_parts[j] = (l, part, t)
                dst = yt[j][:, :, 0:n]
                if part == "attn":
                    use = (l, "O", t)
                    ps = full(use)
                    dve.tensor_tensor(dst, ps[:, 0, :].rearrange("p (c n) -> p c n", n=P)[:, :, 0:n],
                                      za[:, :, START[t]:END[t]], ALU.mult).then_inc(y_made.mark((l, part, t)), 1)
                else:
                    dve.wait_ge(act_took.sem, act_took.at((l, "back", t)))
                    dve.tensor_tensor(dst, sl[t % 2][:, :, 0:n], zc[:, :, START[t]:END[t]], ALU.mult) \
                        .then_inc(y_made.mark((l, part, t)), 1)

            def y_lo(l, part, t):
                n = SIZE[t]
                c = 0 if part == "conv" else CT
                dst = xlo[:, c:c + CT, START[t]:END[t]]
                dve.wait_ge(hi_made.sem, hi_made.at((l, part, t)))
                dve.tensor_tensor(dst, yt[y_slot(l, part, t)][:, :, 0:n],
                                  xhi[:, c:c + CT, START[t]:END[t]].bitcast(F32), ALU.subtract) \
                    .then_inc(lo_made.mark((l, part, t)), 1)

            def residual(l, half, t):
                use = (l, "wo", half, t)
                n = SIZE[t]
                ps = full(use)
                if l == 0 and half == 0:
                    dve.wait_ge(h_loaded, 32)
                dst = h[0:n, t, half * 512:half * 512 + 512]
                dve.scalar_tensor_tensor(dst, dst, ALPHA, ps[0:n, 0, :], ALU.mult, ALU.add) \
                    .then_inc(dve_took.mark(use), 1)
                dve.wait_ge(dve_took.sem, dve_took.at(use))
                dve.bn_stats(stats[0:n, t, half, :], dst).then_inc(dve_step.mark((l, "post", half, t)), 1)

            def post_norm(l, t):
                n = SIZE[t]
                step = (l, "post", t)
                row = h[0:n, t, :]
                dve.wait_ge(dve_step.sem, dve_step.at((l, "post", 1, t)))
                dve.bn_aggr(meanvar[0:n, t, :], stats[0:n, t, :, :].rearrange("p a b -> p (a b)")) \
                    .then_inc(stats_made.mark(step), 1)
                dve.wait_ge(stats_made.sem, stats_made.at(step))
                dve.wait_ge(ln_loaded, 32 * (l + 1))
                dve.scalar_tensor_tensor(row, row, meanvar[0:n, t, 0:1], ln_g[0:n, :], ALU.subtract, ALU.mult) \
                    .then_inc(dve_step.mark((l, "gain", t)), 1)
                dve.wait_ge(dve_step.sem, dve_step.at((l, "gain", t)))
                dve.wait_ge(rstd_made.sem, rstd_made.at(step))
                out = dve.scalar_tensor_tensor(row, row, rstd[0:n, t:t + 1], ln_b[0:n, :], ALU.mult, ALU.add)
                if l < DEPTH - 1:
                    out.then_inc(normed.mark((l, "x", t)), 1)
                    return
                out.then_inc(normed.mark((l, "h", t)), 1)
                dve.wait_ge(normed.sem, normed.at((l, "h", t)))
                if t > 1:
                    dve.wait_ge(psum_full.sem, psum_full.at((l, "xT", t - 1)))
                dve.tensor_tensor_reduce(hn[0][:, :], row, row, 1.0, 0.0, ALU.mult, ALU.add, psums[:, t - 1:t]) \
                    .then_inc(stats_made.mark((2, "in", t)), 1)
                dve.wait_ge(stats_made.sem, stats_made.at((2, "in", t)))
                dve.wait_ge(rstd_made.sem, rstd_made.at((2, "in", t)))
                dve.wait_ge(gain_loaded, 16)
                dve.scalar_tensor_tensor(hn[0][:, :], row, rstd[:, 8 + t:9 + t], gain[:, :], ALU.mult, ALU.mult) \
                    .then_inc(normed.mark((l, "x", t)), 1)

            def x_lo(l, t):
                use = (l, "xT", t)
                n = SIZE[t]
                dve.wait_ge(hi_made.sem, hi_made.at((l, "x", t)))
                src = psum(use)[:, :, :].rearrange("p a (k n) -> p (a k) n", n=P)[:, :, 0:n]
                dve.tensor_tensor(xlo[:, :, START[t]:END[t]], src, xhi[:, :, START[t]:END[t]].bitcast(F32),
                                  ALU.subtract).then_inc(dve_took.mark(use), 1)

            for c in range(4):
                dve.wait_ge(hi_made.sem, hi_made.at((0, "x0", c)))
                dve.tensor_tensor(xlo[:, 2 * c:2 * c + 2, :], xt0[:, 2 * c:2 * c + 2, :],
                                  xhi[:, 2 * c:2 * c + 2, :].bitcast(F32), ALU.subtract) \
                    .then_inc(lo_made.mark((0, "x0", c)), 1)
            dve.wait_ge(consts_loaded, 64)
            dve.wait_ge(small_made.sem, small_made.at("wconv"))
            dve.wait_ge(set_up.sem, set_up.at("mask0"))
            for l in range(DEPTH):
                gate_conv_input(l, 0)
                gate_conv_input(l, 1)
                conv(l, 0, 0, 17)
                gate_conv_input(l, 2)
                gate_conv_input(l, 3)
                conv(l, 0, 17, TAPS)
                for c in range(CT):
                    rope(l, "qi", c)
                rope(l, "ki", 0)
                conv(l, 2, 0, 12)
                add_scores(l)
                todo = [(name, c) for name in ("q", "k") for c in range(CT)]
                topk(l, lambda r: rope(l, *todo.pop(0)) if r >= 2 and (r - 2) % 3 < 2 and todo else None)
                for name, c in todo:
                    rope(l, name, c)
                conv(l, 2, 12, TAPS)
                tiles = list(query_tiles(l))
                for t in tiles:
                    conv_stats(l, t)
                    if t > tiles[0]:
                        conv_norm(l, t - 1)
                conv_norm(l, 4)
                n = len(items[l])
                masked_logits(l, 0)
                for i in range(n):
                    if i + 1 < n:
                        masked_logits(l, i + 1)
                    normalise(l, i)
                    for t in tiles:
                        if i == output_after(l, t):
                            y_part(l, "attn", t)
                        if i == (output_after(l, t) or 0) + 1 and t < 4:
                            y_lo(l, "attn", t)
                for t in tiles:
                    y_part(l, "conv", t)
                    if t > tiles[0]:
                        y_lo(l, "conv", t - 1)
                y_lo(l, "conv", 4)
                y_part(l, "attn", 4)
                y_lo(l, "attn", 4)
                for t in tiles:
                    residual(l, 0, t)
                for t in tiles:
                    residual(l, 1, t)
                    post_norm(l, t)
                    if t > tiles[0]:
                        x_lo(l, t - 1)
                x_lo(l, 4)

            dve.wait_ge(block2_loaded, 8 * 16)

            def gained_tables(dst_c, dst_s, g, factor, name):
                gb = g[:, :].rearrange("p (o d) -> p o d", o=1).broadcast_to([P, 4, HD])
                dve.scalar_tensor_tensor(dst_c[:, :, :], c2[:, :, :], factor, gb, ALU.mult, ALU.mult) \
                    .then_inc(dve_step.mark((2, name, "c")), 1)
                for half in range(2):
                    for s in range(2):
                        a, b = half * AXIAL + s * 16, half * AXIAL + (1 - s) * 16
                        gp = g[:, b:b + 16].rearrange("p (o d) -> p o d", o=1).broadcast_to([P, 4, 16])
                        got = dve.scalar_tensor_tensor(dst_s[:, :, a:a + 16], s2[:, :, a:a + 16], factor, gp,
                                                       ALU.mult, ALU.mult)
                        got.then_inc(dve_step.mark((2, name, half, s)), 1)

            gained_tables(gcq, gsq, qg, SCALE, "q")
            gained_tables(gck, gsk, kg, 1.0, "k")

            def qk_rows(t):
                row, rot = qrow[t % 2], qrot[t % 2]
                dve.wait_ge(act_took.sem, act_took.at((2, "q", t)))
                dve.wait_ge(act_took.sem, act_took.at((2, "kv", t)))
                if t:
                    dve.wait_ge(normed.sem, normed.at((2, "rope", t - 1)))
                dve.tensor_tensor(qtmp[:, :, :], row[:, :, :], row[:, :, :], ALU.mult).then_inc(dve_step.mark((2, "sq", t)), 1)
                dve.wait_ge(dve_step.sem, dve_step.at((2, "sq", t)))
                if t:
                    dve.wait_ge(rstd_made.sem, rstd_made.at((2, "qk", t - 1)))
                dve.tensor_reduce(veps[:, 0:10], qtmp[:, :, :], mybir.AxisListType.X, ALU.add) \
                    .then_inc(stats_made.mark((2, "qk", t)), 1)
                dve.wait_ge(rstd_made.sem, rstd_made.at((2, "qk", t)))
                r = rstd[:, 0:10].rearrange("p (h o) -> p h o", o=1).broadcast_to([P, 10, HD])
                dve.tensor_tensor(row[:, :, :], row[:, :, :], r, ALU.mult).then_inc(dve_step.mark((2, "unit", t)), 1)
                dve.wait_ge(dve_step.sem, dve_step.at((2, "unit", t)))
                if t >= 2:
                    dve.wait_ge(psum_full.sem, psum_full.at((2, "qkT", t - 2)))
                for h0, h1, gc, gs in ((0, 8, gcq, gsq), (8, 10, gck, gsk)):
                    nh = h1 - h0
                    cb = gc[:, t, :].rearrange("p (o d) -> p o d", o=1).broadcast_to([P, nh, HD])
                    dve.tensor_tensor(rot[:, h0:h1, :], row[:, h0:h1, :], cb, ALU.mult)
                    for half in range(2):
                        for s in range(2):
                            a, b = half * AXIAL + s * 16, half * AXIAL + (1 - s) * 16
                            sb_ = gs[:, t, a:a + 16].rearrange("p (o d) -> p o d", o=1).broadcast_to([P, nh, 16])
                            got = dve.tensor_tensor(qtmp[:, h0:h1, a:a + 16], row[:, h0:h1, b:b + 16], sb_, ALU.mult)
                got.then_inc(normed.mark((2, "qk", t)), 1)
                dve.wait_ge(normed.sem, normed.at((2, "qk", t)))
                dve.tensor_tensor(rot[:, :, :], rot[:, :, :], qtmp[:, :, :], ALU.add).then_inc(normed.mark((2, "rope", t)), 1)

            def v_rows(t):
                step = (2, "v", t)
                row = gv[t % 2]
                dve.wait_ge(act_took.sem, act_took.at((2, "vin", t)))
                dve.bn_stats(stats[:, t, 0, :], row[:, :]).then_inc(dve_step.mark(step), 1)
                dve.wait_ge(dve_step.sem, dve_step.at(step))
                dve.bn_aggr(meanvar[:, t, :], stats[:, t, 0, :]).then_inc(stats_made.mark(step), 1)
                dve.wait_ge(stats_made.sem, stats_made.at(step))
                dve.scalar_tensor_tensor(row[:, :], row[:, :], meanvar[:, t, 0:1], lnv_g[:, :], ALU.subtract, ALU.mult) \
                    .then_inc(dve_step.mark((2, "vg", t)), 1)
                dve.wait_ge(dve_step.sem, dve_step.at((2, "vg", t)))
                dve.wait_ge(rstd_made.sem, rstd_made.at(step))
                dve.scalar_tensor_tensor(vv[:, t, :], row[:, :], rstd[:, 12 + t:13 + t], lnv_b[:, :], ALU.mult, ALU.add) \
                    .then_inc(normed.mark(step), 1)

            def u_rows(t):
                dve.wait_ge(act_took.sem, act_took.at((2, "gb", t)))
                dve.wait_ge(act_took.sem, act_took.at((2, "u", t)))
                dve.tensor_tensor(ug[:, t, :], ug[:, t, :], sgb[t % 2][:, :], ALU.mult).then_inc(normed.mark((2, "ug", t)), 1)

            def mlp_gate(pair_):
                use = (2, "vmix", pair_)
                ps = full(use)
                for i in range(2):
                    g = 2 * pair_ + i
                    dst = ug[:, :, g * GD:g * GD + GD]
                    got = dve.scalar_tensor_tensor(dst, ps[:, i, 0:4 * GD].rearrange("p (t d) -> p t d", t=4),
                                                   vec[:, V_BSPAT + g:V_BSPAT + g + 1], dst, ALU.add, ALU.mult)
                got.then_inc(dve_took.mark(use), 1)

            def mlp_lo(t):
                use = (2, "gmT", t)
                dve.wait_ge(hi_made.sem, hi_made.at((2, "gm", t)))
                c0, c1 = P * t, P * t + P
                dve.tensor_tensor(xlo[:, CT:2 * CT, c0:c1], psum(use)[:, 0, :].rearrange("p (c n) -> p c n", n=P),
                                  xhi[:, CT:2 * CT, c0:c1].bitcast(F32), ALU.subtract).then_inc(dve_took.mark(use), 1)

            def max2(i):
                t, hd = items2[i]
                ps = full((2, "S2", t, hd))
                if i >= 4:
                    dve.wait_ge(act_took.sem, act_took.at((2, "S2", *items2[i - 4])))
                dve.tensor_reduce(nmax[:, i % 4:i % 4 + 1], ps[:, 0, :], mybir.AxisListType.X, ALU.max, negate=True) \
                    .then_inc(rsum_made.mark((2, "max", i)), 1)

            def normalise2(i):
                t, hd = items2[i]
                dve.wait_ge(act_took.sem, act_took.at((2, "S2", t, hd)))
                dve.reciprocal(rsums[:, i % 4:i % 4 + 1], psums[:, i % 4:i % 4 + 1]).then_inc(rsum_made.mark((2, i)), 1)
                dve.wait_ge(rsum_made.sem, rsum_made.at((2, i)))
                dve.tensor_scalar(e2[i % 3][:, :], e2[i % 3][:, :], rsums[:, i % 4:i % 4 + 1], None, ALU.mult) \
                    .then_inc(probs_made.mark((2, i)), 1)

            def attn2_part(t):
                use = (2, "O2", t)
                dve.wait_ge(psum_full.sem, psum_full.at((2, "PV2", t, HEADS - 1)))
                if t >= 2:
                    dve.wait_ge(lo_made.sem, lo_made.at((2, "attn", t - 2)))
                dve.tensor_tensor(yt2[t % 2][:, :].rearrange("p (c n) -> p c n", n=P),
                                  psum(use)[:, 0, :].rearrange("p (c n) -> p c n", n=P),
                                  sga[:, :, P * t:P * t + P], ALU.mult).then_inc(y_made.mark((2, "attn", t)), 1)

            def attn2_lo(t):
                dve.wait_ge(hi_made.sem, hi_made.at((2, "attn", t)))
                c0, c1 = P * t, P * t + P
                dve.tensor_tensor(xlo[:, 0:CT, c0:c1], yt2[t % 2][:, :].rearrange("p (c n) -> p c n", n=P),
                                  xhi[:, 0:CT, c0:c1].bitcast(F32), ALU.subtract).then_inc(lo_made.mark((2, "attn", t)), 1)

            def merge(d):
                ya, yb = (2, "ya", d), (2, "yb", d)
                ps = full(ya)
                if d >= 2:
                    dve.wait_ge(lo_made.sem, lo_made.at((2, "y", d - 2)))
                dst = yt2[d % 2][:, :]
                dve.scalar_tensor_tensor(tg[:, d, :], tg[:, d, :], 1.0, ps[:, 0, :], ALU.add, ALU.mult) \
                    .then_inc(dve_took.mark(ya), 1)
                ps = full(yb)
                dve.scalar_tensor_tensor(tg[:, KD + d, :], tg[:, KD + d, :], 1.0, ps[:, 0, :], ALU.add, ALU.mult) \
                    .then_inc(dve_took.mark(yb), 1)
                dve.wait_ge(dve_took.sem, dve_took.at(yb))
                dve.tensor_tensor(dst, tg[:, d, :], tg[:, KD + d, :], ALU.add).then_inc(y_made.mark((2, "y", d)), 1)

            def merge_lo(d):
                dve.wait_ge(hi_made.sem, hi_made.at((2, "y", d)))
                dve.tensor_tensor(y2lo[:, d, :], yt2[d % 2][:, :], y2hi[:, d, :].bitcast(F32), ALU.subtract) \
                    .then_inc(lo_made.mark((2, "y", d)), 1)

            def last_residual(half, t):
                use = (2, "wo", half, t)
                ps = full(use)
                dst = h[:, t + 1, half * 512:half * 512 + 512]
                dve.scalar_tensor_tensor(dst, ps[:, 0, :], 0.5, dst, ALU.mult, ALU.add).then_inc(dve_took.mark(use), 1)

            def last_norm(t):
                dve.wait_ge(rstd_made.sem, rstd_made.at(("out", t)))
                dve.scalar_tensor_tensor(h[:, t + 1, :], h[:, t + 1, :], rstd[:, t:t + 1], fgain[:, :], ALU.mult, ALU.mult) \
                    .then_inc(normed.mark(("out", t)), 1)

            for t in range(4):
                qk_rows(t)
            for t in range(4):
                v_rows(t)
            for t in range(4):
                u_rows(t)
            for pair_ in range(4):
                mlp_gate(pair_)
            for t in range(4):
                mlp_lo(t)
            n = len(items2)
            max2(0)
            for i in range(n):
                if i + 1 < n:
                    max2(i + 1)
                normalise2(i)
                for t in range(3):
                    if i == output2_after(t):
                        attn2_part(t)
                    if i == output2_after(t) + 1:
                        attn2_lo(t)
            attn2_part(3)
            attn2_lo(3)
            for d in range(KD):
                merge(d)
                if d:
                    merge_lo(d - 1)
            merge_lo(KD - 1)
            for t in range(4):
                last_residual(0, t)
            for t in range(4):
                last_residual(1, t)
                if t:
                    last_norm(t - 1)
            last_norm(3)

        out = {name: s.steps for name, s in signals.items()}
        out["psum"] = psum_of
    return out


def rope_tables():
    freq = np.float32(THETA) ** (-np.arange(0, HD, 2, dtype=np.float32) / np.float32(HD))
    ang = np.arange(L, dtype=np.float32)[:, None] * freq[None, :]
    c, s = np.cos(ang).T, np.sin(ang).T
    return (np.ascontiguousarray(np.concatenate([c, c, c, c], 0), np.float32),
            np.ascontiguousarray(np.concatenate([-s, s, -s, s], 0), np.float32))


def axial_tables():
    freq = np.float32(THETA) ** (-np.arange(0, AXIAL, 2, dtype=np.float32) / np.float32(AXIAL))
    pos = np.arange(SEQ)
    parts_c, parts_s = [], []
    for where in (pos // GRID_W, pos % GRID_W):
        ang = where.astype(np.float32)[:, None] * freq[None, :]
        c, s = np.cos(ang), np.sin(ang)
        parts_c += [c, c]
        parts_s += [-s, s]
    c, s = (np.concatenate(x, 1).astype(np.float32).reshape(4, P, HD).transpose(1, 0, 2) for x in (parts_c, parts_s))
    return np.ascontiguousarray(c), np.ascontiguousarray(s)


def column_block(w, c0, width):
    out = np.zeros((P, BLOCK), w.dtype)
    out[:, 0:KD * width] = w[:, c0:c0 + width].reshape(KD, P, width).transpose(1, 0, 2).reshape(P, KD * width)
    return out


def half_block(w, half, c0):
    return w[half * 512:half * 512 + 512, c0:c0 + 512].reshape(4, P, 512).transpose(1, 0, 2).reshape(P, BLOCK)


def pack_weights(i):
    sizes = [512, 512, 512, 512, 512, 512, 512, 512, 64, 8]
    names = ["a", "g", "zc", "q", "k", "v", "za", "qi", "ki", "wi"]
    at = dict(zip(names, np.cumsum([0] + sizes)))
    names2 = ["q", "kv", "ga", "u", "vin", "gb", "gm"]
    at2 = dict(zip(names2, np.cumsum([0, 512, 256, 512, 512, 512, 512])))
    out = np.empty((len(BLOCKS), P, BLOCK), np.asarray(i["w_in"]).dtype)
    for n, (key, _, _) in enumerate(BLOCKS):
        l, name, x = key[0], key[1], key[2]
        if l < DEPTH:
            w = i["w_in"][l]
            if name == "wo":
                out[n] = half_block(i["w_out"][l], key[3], 512 * x)
            elif name == "v":
                out[n] = half_block(w, x, at["v"])
            elif name == "ki":
                out[n] = column_block(w, at["ki"], HD + HEADS)
            else:
                out[n] = column_block(w, at[name] + P * x, 2 * P)
        else:
            w = i["w_in_2"][0]
            if name == "wo":
                out[n] = half_block(i["w_out_2"][0], key[3], 512 * x)
            elif name in ("ya", "yb"):
                out[n] = half_block(i["w_proj_attn_2" if name == "ya" else "w_proj_gmlp_2"][0], 0, P * x)
            elif name in ("q", "vin", "u", "gb"):
                out[n] = half_block(w, x, at2[name])
            else:
                out[n] = column_block(w, at2[name] + P * x, 2 * P)
    return out


def pack_vectors(i):
    rows = [np.asarray(i["conv_w"]).reshape(-1, P)]
    for name in ("conv_b", "conv_ln_g", "conv_ln_b"):
        rows.append(np.asarray(i[name]).reshape(-1, P))
    rows.append(np.asarray(i["b_merge_2"]).reshape(-1, P))
    rows.append(np.asarray(i["b_spatial_2"]).reshape(-1, P))
    return np.ascontiguousarray(np.concatenate(rows, 0).T)


def kernel(**inputs):
    import concourse.bacc as bacc
    from concourse.bass_utils import run_bass_kernel_spmd as run

    i = {name: np.asarray(a) for name, a in inputs.items()}
    rope_cos, rope_sin = rope_tables()
    axial_cos, axial_sin = axial_tables()
    rows = np.concatenate([i["meta_tokens"], i["x"][0]], 0)
    arrays = {
        "weights": pack_weights(i),
        "vectors": pack_vectors(i),
        "x_t": np.ascontiguousarray(rows.T.reshape(KD, P, L).transpose(1, 0, 2)),
        "w_spatial_t": np.ascontiguousarray(i["w_spatial_2"][0].transpose(2, 0, 1)),
        "identity": np.eye(P, dtype=np.float32),
        "rope_cos": rope_cos, "rope_sin": rope_sin, "axial_cos": axial_cos, "axial_sin": axial_sin,
    }
    for name in ("x", "meta_tokens", "post_ln_g", "post_ln_b", "norm_gain_2", "q_gain_2", "k_gain_2",
                 "ln_v_gain_2", "ln_v_bias_2", "final_gain_2"):
        arrays[name] = np.ascontiguousarray(i[name])

    def program(counted):
        nc = bacc.Bacc("TRN2", target_bir_lowering=False, num_devices=1, dynamic_dma_scratch_size=1024)
        io = {name: nc.dram_tensor(f"in_{name}", a.shape, mybir.dt.from_np(a.dtype), kind="ExternalInput").ap()
              for name, a in arrays.items()}
        io["out"] = nc.dram_tensor("out_0", (1, SEQ, D), F32, kind="ExternalOutput").ap()
        return nc, build(nc, io, counted)

    _, counted = program(None)
    nc, again = program(counted)
    assert again == counted
    r = run(nc, [{f"in_{name}": a for name, a in arrays.items()}], core_ids=[0])
    return r.results[0]["out_0"]
```

```python
from contextlib import ExitStack

import numpy as np

import concourse.bass as bass
from concourse import mybir

ALU = mybir.AluOpType
ACT = mybir.ActivationFunctionType
F32 = mybir.dt.float32
F32R = mybir.dt.float32r
BF16 = mybir.dt.bfloat16

P = 128
D = 1024
KD = D // P
SEQ = 512
META = 16
L = META + SEQ
PAD = 30
TAPS = PAD + 1
DC = 512
CT = DC // P
HEADS = 8
HD = 64
TOPK = 132
DEPTH = 2
ALPHA = (2.0 * DEPTH) ** 0.25
LN_EPS = 1e-5
EPS = 1e-6
SCALE = HD ** -0.5
IDX_SCALE = HD ** -0.5
IDX_W_SCALE = HEADS ** -0.5
THETA = 10000.0
GRID_W = 64
AXIAL = HD // 2
GROUPS = 8
GD = DC // GROUPS

START = [0, 16, 144, 272, 400]
SIZE = [16, 128, 128, 128, 128]
END = [s + n for s, n in zip(START, SIZE)]
TILES = range(5)
MAIN = range(1, 5)
SCORE_AT = [None, 0, 144, 416, 816]
SCORES = 816 + END[4]
MASK0_AT = SCORES

FILL = -3.0e38
MARK = -3.3e38
HIDE = -1.0e30

BLOCK = 2048
RING = 4
PASSES = ((0, 0), (0, 1), (1, 0))


def query_tiles(l):
    return TILES if l == 0 else MAIN


def column_halves(first):
    mid = first + (L - first) // 2
    return (first, mid), (mid, L)


def weight_stream():
    blocks, uses = [], []

    def pairs(l, *names):
        for name in names:
            for c in (0, 2):
                blocks.append(((l, name, c), BLOCK, (l, name, c + 1)))
            uses.extend((l, name, c) for c in range(CT))

    def halves(l, name, tiles):
        for half in range(2):
            blocks.append(((l, name, half), BLOCK, (l, name, tiles[-1])))
        uses.extend((l, name, t) for t in tiles)

    def output(l, tiles):
        for n in range(2):
            for half in range(2):
                blocks.append(((l, "wo", n, half), BLOCK, (l, "wo", n, tiles[-1])))
            uses.extend((l, "wo", n, t) for t in tiles)

    for l in range(DEPTH):
        for c in (0, 2):
            for name in ("a", "g"):
                blocks.append(((l, name, c), BLOCK, (l, name, c + 1)))
                uses.extend([(l, name, c), (l, name, c + 1)])
        pairs(l, "qi")
        blocks.append(((l, "ki", 0), KD * (HD + HEADS), (l, "ki", 0)))
        uses.append((l, "ki", 0))
        pairs(l, "zc", "q", "k")
        halves(l, "v", TILES)
        for c in (0, 2):
            blocks.append(((l, "za", c), BLOCK, (l, "za", c + 1, 1)))
        uses.extend((l, "za", c, half) for half in range(2) for c in range(CT))
        output(l, query_tiles(l))
    l = DEPTH
    halves(l, "q", range(4))
    blocks.append(((l, "kv", 0), BLOCK, (l, "kv", 3)))
    uses.extend((l, "kv", t) for t in range(4))
    for name in ("vin", "u", "gb"):
        halves(l, name, range(4))
    pairs(l, "ga")
    for c in range(0, 2 * KD, 2):
        blocks.append(((l, "gm", c), BLOCK, (l, "gm", c + 1)))
        uses.extend([(l, "gm", c), (l, "gm", c + 1)])
    for d in (0, 4):
        for name in ("yb", "ya"):
            blocks.append(((l, name, d), BLOCK, (l, name, d + 3)))
        uses.extend((l, name, d + i) for i in range(4) for name in ("yb", "ya"))
    output(l, range(4))
    return blocks, uses


BLOCKS, USES = weight_stream()
NUMBER = {key: n for n, (key, _, _) in enumerate(BLOCKS)}
SPLIT_AT = {}
for _n in range(RING, len(BLOCKS)):
    _at = USES.index(BLOCKS[_n - RING][2]) + 1
    if USES[_at] in SPLIT_AT and USES[_at][1] != "wo":
        _at += 1
    SPLIT_AT.setdefault(USES[_at], []).append(_n)


V_CONVW = 0
V_CONVB = V_CONVW + DEPTH * TAPS * CT
V_CLNG = V_CONVB + DEPTH * CT
V_CLNB = V_CLNG + DEPTH * CT
V_BMERGE = V_CLNB + DEPTH * CT
V_BSPAT = V_BMERGE + 2 * KD
V_COUNT = V_BSPAT + GROUPS


def attention_items(l):
    return [(t, hd) for t in query_tiles(l) for hd in range(HEADS)]


TAPS_AHEAD = 15


def attention_extras(l):
    tiles = list(query_tiles(l))
    n = len(attention_items(l))
    todo = {engine: [[] for _ in range(n)] for engine in ("pe", "act", "dve_first", "dve", "pool")}
    for i in range(8):
        gate = ("za", i % CT, i // CT)
        todo["pe"][i].append(gate)
        todo["act"][i].append(gate)
        todo["dve"][i + 1].append(gate)
    i = 0
    for tap in range(TAPS_AHEAD, TAPS, 2):
        todo["dve"][i].append(("taps", tap, tap + 2))
        i += 1
    i += 2
    for t in tiles:
        todo["pe"][i].append(("fwd", t))
        todo["dve"][i + 1].append(("stats", t))
        todo["pool"][i + 1].append(("deviation", t))
        todo["dve"][i + 2].append(("norm", t))
        todo["pe"][i + 3].append(("back", t))
        todo["act"][i + 3].append(("affine", t))
        todo["dve"][i + 5].append(("y", "conv", t))
        todo["act"][i + 5].append(("hi", "conv", t))
        todo["pool"][i + 5].append(("lo", "conv", t))
        i += 4
    for j, t in enumerate(tiles[:-1]):
        i = (j + 1) * HEADS + 1
        todo["dve_first"][i].append(("y", "attn", t))
        todo["act"][i].append(("hi", "attn", t))
        todo["pool"][i + 1].append(("lo", "attn", t))
    return todo


Y_SLOT = {"attn": 0, "conv": 1}


class Signal:

    def __init__(self, sem, counted):
        self.sem = sem
        self.counted = counted
        self.steps = {}

    def mark(self, step):
        assert step not in self.steps, step
        self.steps[step] = len(self.steps) + 1
        return self.sem

    def at(self, step):
        if self.counted is None:
            return 1
        return self.counted[step]


def build(nc, io, counted):
    with ExitStack() as ctx:
        signals = {}
        known_bufs = counted["psum"] if counted else None
        psum_of = {}

        def signal(name):
            s = Signal(ctx.enter_context(nc.semaphore(name)), counted[name] if counted else None)
            signals[name] = s
            return s

        where = [1152]

        def sb(name, shape, dtype=F32, at=None):
            size = 2 if dtype == BF16 else 4
            n = size
            for s in shape[1:]:
                n *= s
            n = -(-n // 32) * 32
            offset = where[0] if at is None else at
            if at is None:
                where[0] += n
            return nc.alloc_sbuf_tensor_at(name, shape, dtype, offset=offset)

        whi = [sb(f"w_hi{i}", [P, BLOCK], F32R) for i in range(RING)]
        RAW_AT = where[0]
        raw = [sb(f"w_raw{i}", [P, BLOCK]) for i in range(RING)]
        wlo = [sb(f"w_lo{i}", [P, BLOCK], F32R, at=RAW_AT + 4 * BLOCK * i) for i in range(RING)]
        xhi = sb("x_hi", [P, KD, L], F32R)
        xlo = sb("x_lo", [P, KD, L], F32R)
        H_AT = where[0]
        h = sb("h", [P, 5, D])
        ident = sb("ident", [P, P])
        COS_AT = where[0]
        cos = sb("cos", [P, L])
        sin = sb("sin", [P, L])
        vec = sb("vec", [P, V_COUNT])
        bmerge = sb("b_merge_half", [P, 2 * KD])
        widx = sb("w_idx", [P, 4, HEADS])
        stats = sb("stats", [P, 5, 2, 6])
        meanvar = sb("meanvar", [P, 5, 2])
        veps = sb("var_eps", [P, 16])
        rstd = sb("rstd", [P, 16])
        squares = sb("qk_squares", [P, 4, 10])
        unit = sb("qk_unit", [P, 4, 10])
        minus_half = sb("minus_half", [P, 16])
        top8 = sb("top8", [P, 4, 8])
        nmax = sb("neg_max", [P, 4])
        psums = sb("prob_sums", [P, 4])
        rsums = sb("prob_rsums", [P, 4])
        BLOCK2_AT = where[0]
        U_AT = where[0]
        u = sb("u", [P, CT, 560])
        acc = sb("conv_acc", [P, CT, L])
        zc = sb("zc", [P, CT, L])
        QI_AT = where[0]
        qi = sb("q_idx", [P, CT, L])
        za = sb("za", [P, CT, L], at=QI_AT)
        Q_AT = where[0]
        q = sb("q", [P, CT, L])
        relu = [sb(f"relu{i}", [P, L], at=Q_AT + 4 * L * i) for i in range(8)]
        K_AT = where[0]
        k = sb("k", [P, CT, L])
        xt0 = sb("x_first", [P, KD, L], at=Q_AT)
        ln_g = sb("post_ln_g", [P, D], at=Q_AT)
        ln_b = sb("post_ln_b", [P, D], at=Q_AT + 4 * D)
        gain = sb("norm_gain", [P, D], at=K_AT)
        hn = [sb("h_normed0", [P, D], at=K_AT + 4 * D), sb("h_normed1", [P, D], at=where[0])]
        v = sb("v", [P, 5, DC])
        XS_AT = where[0]
        xs = [sb(f"shifted{i}", [P, L]) for i in range(4)]
        cnorm = [None] + [sb(f"conv_normed{t}", [P, DC], at=XS_AT + 2048 * (t - 1)) for t in MAIN]
        SC_AT = where[0]
        score = sb("score", [P, SCORES])
        pt = [sb(f"probs_t{i}", [P, 640], at=SC_AT + 2560 * i) for i in range(2)]
        square = sb("square", [P, D], at=SC_AT)
        KI_AT = where[0]
        ki = sb("k_idx", [P, L])
        mask = sb("mask", [P, SCORES + 16], BF16)
        WIT_AT = where[0]
        wit = sb("w_idx_t", [P, L])
        e = [sb(f"exps{i}", [P, L]) for i in range(4)]
        yt = [sb(f"y_part{i}", [P, CT, P]) for i in range(2)]
        sl = [sb(f"conv_affine{i}", [P, CT, P]) for i in range(2)]
        th = [sb("conv_tanh0", [P, CT, P], at=KI_AT), sb("conv_tanh1", [P, CT, P])]
        cnorm[0] = sb("conv_normed0", [P, DC], at=WIT_AT)
        assert where[0] <= nc.sbuf_usable_end, where[0]

        where[0] = BLOCK2_AT
        v2 = sb("v2", [P, 4, 2 * HD])
        k2_hi = sb("k2_hi", [P, 2, SEQ], F32R)
        TABLES_AT = where[0]
        c2 = sb("axial_cos", [P, 4, HD])
        s2 = sb("axial_sin", [P, 4, HD])
        qg = sb("q_gain", [P, HD])
        kg = sb("k_gain", [P, HD])
        wst = sb("w_spatial_t", [P, GROUPS, P])
        lnv_g = sb("ln_v_g", [P, DC])
        lnv_b = sb("ln_v_b", [P, DC])
        gcq = sb("cos_gain_q", [P, 4, HD])
        gsq = sb("sin_gain_q", [P, 4, HD])
        gck = sb("cos_gain_k", [P, 4, HD])
        gsk = sb("sin_gain_k", [P, 4, HD])
        e2 = [sb(f"exps2_{i}", [P, SEQ], at=COS_AT + 2048 * i if i < 2 else TABLES_AT) for i in range(3)]
        pt2 = [sb(f"probs2_t{i}", [P, SEQ], at=TABLES_AT + 2048 * (1 + i)) for i in range(2)]
        yt2 = [sb(f"y2_part{i}", [P, SEQ], at=TABLES_AT + 2048 * (3 + i)) for i in range(2)]
        assert 4096 <= 2 * 4 * L
        where[0] = QI_AT - 4 * CT * SEQ
        assert where[0] >= TABLES_AT + 2048 * 5
        attn_lo = sb("attn2_lo", [P, CT, SEQ], F32R)
        q2 = [sb("q2_first", [P, CT, 2, 2, P], F32R, at=QI_AT - 4 * CT * SEQ), sb("q2_last", [P, CT, 2, 2, P], F32R)]
        assert where[0] == QI_AT + 4 * CT * SEQ
        sga = sb("silu_gate_a", [P, CT, SEQ])
        ug = sb("u_gated", [P, 4, DC])
        vv = sb("v_normed", [P, 4, DC])
        attn_hi = sb("attn2_hi", [P, CT, SEQ], F32R, at=where[0] - 4 * CT * SEQ * 2)
        mlp_hi = sb("mlp_hi", [P, CT, SEQ], F32R, at=where[0] - 4 * CT * SEQ)
        mlp_lo = sb("mlp_lo", [P, CT, SEQ], F32R)
        TG_AT = where[0]
        tg = sb("merge_tanh", [P, 2 * KD, SEQ])
        sgb = [sb(f"silu_gate_b{i}", [P, DC], at=TG_AT + 2048 * i) for i in range(4)]
        qrow = [sb(f"qk_row{i}", [P, 10, HD], at=TG_AT + 8192 + 2560 * i) for i in range(4)]
        qrot = [sb(f"qk_rot{i}", [P, 10, HD], at=TG_AT + 8192 + 2560 * (4 + i)) for i in range(4)]
        assert TG_AT + 8192 + 2560 * 8 <= TG_AT + 2048 * (2 * KD - 2)
        k2_lo = sb("k2_lo", [P, 2, SEQ], F32R, at=TG_AT + 2048 * (2 * KD - 2))
        qtmp = sb("qk_tmp", [P, 10, HD], at=TG_AT - 4 * CT * SEQ)
        assert where[0] <= nc.sbuf_usable_end, where[0]
        fgain = sb("final_gain", [P, D], at=H_AT)

        bank = {x: ctx.enter_context(nc.psum_tensor(f"psum_{x}", [P, 2, 512], F32)) for x in "ABCD"}

        def psum(use):
            name, first = known_bufs[use] if known_bufs else ("A", 0)
            return bank[name][:, first:2, :]

        raw_loaded = [ctx.enter_context(nc.semaphore(f"raw_loaded{i}")) for i in range(RING)]
        consts_loaded = ctx.enter_context(nc.semaphore("consts_loaded"))
        xt0_loaded = [ctx.enter_context(nc.semaphore(f"xt0_loaded{i}")) for i in range(4)]
        h_loaded = ctx.enter_context(nc.semaphore("h_loaded"))
        ln_loaded = ctx.enter_context(nc.semaphore("ln_loaded"))
        gain_loaded = ctx.enter_context(nc.semaphore("gain_loaded"))
        block2_loaded = ctx.enter_context(nc.semaphore("block2_loaded"))
        stored = ctx.enter_context(nc.semaphore("stored"))
        weights_hi = signal("weights_hi")
        weights_lo = signal("weights_lo")
        psum_full = signal("psum_full")
        act_took = signal("act_took")
        dve_took = signal("dve_took")
        hi_made = signal("hi_made")
        lo_made = signal("lo_made")
        part_lo = signal("part_lo")
        exp_made = signal("exp_made")
        small_made = signal("small_made")
        u_made = signal("u_made")
        tap_done = signal("tap_done")
        rope_cos = signal("rope_cos")
        rope_sin = signal("rope_sin")
        rope_made = signal("rope_made")
        score_added = signal("score_added")
        causal_done = signal("causal_done")
        topk_max = signal("topk_max")
        topk_marked = signal("topk_marked")
        mask_made = signal("mask_made")
        rsum_made = signal("rsum_made")
        probs_made = signal("probs_made")
        y_made = signal("y_made")
        stats_made = signal("stats_made")
        dve_step = signal("dve_step")
        rstd_made = signal("rstd_made")
        pool_step = signal("pool_step")
        set_up = signal("set_up")
        normed = signal("normed")

        TAKEN_BY_DVE = {"za", "fwd", "S", "wo", "xT", "vmix", "gmT", "ya", "yb", "qkT"}

        def taken(use):
            if use[1] in ("O", "O2"):
                return y_made.sem, y_made.at((use[0], "attn", use[2]))
            by = dve_took if use[1] in TAKEN_BY_DVE else act_took
            return by.sem, by.at(use)

        items = {l: attention_items(l) for l in range(DEPTH)}
        extras = {l: attention_extras(l) for l in range(DEPTH)}
        items2 = [(t, hd) for t in range(4) for hd in range(HEADS)]

        block = ctx.enter_context(nc.Block())

        @block.sync
        def _(sp):
            def load_weights(n):
                key, width, _ = BLOCKS[n]
                if n >= RING:
                    sp.wait_ge(psum_full.sem, psum_full.at(BLOCKS[n - RING][2]))
                sp.dma_start(raw[n % RING][:, 0:width], io["weights"][n, :, 0:width]) \
                    .then_inc(raw_loaded[n % RING], 16)

            def load_first_x(c):
                sp.dma_start(xt0[:, 2 * c:2 * c + 2, :], io["x_t"][:, 2 * c:2 * c + 2, :]) \
                    .then_inc(xt0_loaded[c], 16)

            def row(ap, n):
                return ap.rearrange("(o n) -> o n", o=1).broadcast_to([P, n])

            def load_post_ln(l):
                sp.wait_ge(psum_full.sem, psum_full.at((l, "O", 4)))
                sp.dma_start(ln_g[:, :], row(io["post_ln_g"][l], D)).then_inc(ln_loaded, 16)
                sp.dma_start(ln_b[:, :], row(io["post_ln_b"][l], D)).then_inc(ln_loaded, 16)
                if l == DEPTH - 1:
                    sp.dma_start(gain[:, :], row(io["norm_gain_2"][0], D)).then_inc(gain_loaded, 16)

            def load_block2():
                sp.wait_ge(psum_full.sem, psum_full.at((DEPTH - 1, "fwd", 4)))
                for dst, src in (
                    (c2[:, :, :], io["axial_cos"]), (s2[:, :, :], io["axial_sin"]),
                    (qg[:, :], row(io["q_gain_2"][0], HD)), (kg[:, :], row(io["k_gain_2"][0], HD)),
                    (wst[:, :, :], io["w_spatial_t"]),
                    (lnv_g[:, :], row(io["ln_v_gain_2"][0], DC)),
                    (lnv_b[:, :], row(io["ln_v_bias_2"][0], DC)),
                    (fgain[:, :], row(io["final_gain_2"], D)),
                ):
                    sp.dma_start(dst, src).then_inc(block2_loaded, 16)

            load_first_x(0)
            load_weights(0)
            for c in range(1, 4):
                load_first_x(c)
            load_weights(1)
            for dst, src in ((vec[:, :], io["vectors"]), (cos[:, :], io["rope_cos"]),
                             (sin[:, :], io["rope_sin"]), (ident[:, :], io["identity"])):
                sp.dma_start(dst, src).then_inc(consts_loaded, 16)
            for n in range(2, len(BLOCKS)):
                key = BLOCKS[n][0]
                if key == (0, "v", 0):
                    sp.dma_start(h[0:META, 0, :], io["meta_tokens"]).then_inc(h_loaded, 16)
                    sp.dma_start(h[:, 1:5, :], io["x"][0].rearrange("(t p) d -> p t d", p=P)).then_inc(h_loaded, 16)
                if key == (1, "a", 0):
                    load_post_ln(0)
                if key == (2, "q", 0):
                    load_block2()
                    load_post_ln(1)
                load_weights(n)
            for t in range(4):
                sp.wait_ge(normed.sem, normed.at(("out", t)))
                sp.dma_start(io["out"][0, P * t:P * t + P, :], h[:, t + 1, :]).then_inc(stored, 16)
            sp.wait_ge(stored, 64)

        @block.scalar
        def _(act):
            def split_hi(n, part=None):
                width = BLOCKS[n][1]
                a, b = {None: (0, width), 0: (0, width // 2), 1: (width // 2, width)}[part]
                act.wait_ge(raw_loaded[n % RING], 16 * (n // RING + 1))
                got = act.activation(whi[n % RING][:, a:b], raw[n % RING][:, a:b], ACT.Copy)
                if part != 0:
                    got.then_inc(weights_hi.mark(n), 1)

            def next_blocks(use):
                for n in SPLIT_AT.get(use, []):
                    split_hi(n)

            def full(use):
                act.wait_ge(psum_full.sem, psum_full.at(use))
                return psum(use)

            def halves(use, first):
                n = (L - first) // 2
                return full(use)[:, 0:2, 0:n], first

            def pair(ap):
                return ap.rearrange("p (a b) -> p a b", a=2)

            shift_uses = []

            def shift_buffer(step):
                n = len(shift_uses)
                if n >= 4:
                    sig, prev = shift_uses[n - 4]
                    act.wait_ge(sig.sem, sig.at(prev))
                return xs[n % 4]

            def take_channels(l, name, c):
                use = (l, name, c)
                first = META if l and name in ("zc", "za", "q", "qi") else 0
                ps, _ = halves(use, first)
                if name == "a":
                    if l == 1:
                        act.wait_ge(tap_done.sem, tap_done.at((0, c, TAPS - 1)))
                    act.activation(pair(u[:, c, PAD:PAD + L]), ps, ACT.Copy, scale=0.5).then_inc(act_took.mark(use), 1)
                elif name == "g":
                    buf = shift_buffer(use)
                    act.activation(pair(buf[:, :]), ps, ACT.Tanh, scale=0.5).then_inc(act_took.mark(use), 1)
                    shift_uses.append((u_made, (l, c)))
                elif name == "zc":
                    if l == 1:
                        act.wait_ge(y_made.sem, y_made.at((0, "conv", 4)))
                    act.activation(pair(zc[:, c, first:L]), ps, ACT.Silu).then_inc(act_took.mark(use), 1)
                else:
                    dst = {"qi": qi, "q": q, "k": k}[name]
                    if name == "qi" and l == 1 and c == 0:
                        act.wait_ge(y_made.sem, y_made.at((0, "attn", 4)))
                    if name == "q" and c == 0:
                        act.wait_ge(score_added.sem, score_added.at((l, HEADS - 1, 4)))
                    buf = shift_buffer(use)
                    act.activation(pair(dst[:, c, first:L]), ps, ACT.Copy)
                    for s in range(4):
                        o = 32 * (s ^ 1)
                        got = act.activation(pair(buf[32 * s:32 * s + 32, first:L]), ps[o:o + 32], ACT.Copy)
                    got.then_inc(act_took.mark(use), 1)
                    shift_uses.append((rope_made, use))
                if name != "zc":
                    next_blocks(use)

            def take_index_keys(l):
                use = (l, "ki", 0)
                ps, _ = halves(use, 0)
                buf = shift_buffer(use)
                if l == 1:
                    act.wait_ge(psum_full.sem, psum_full.at((0, "idx", HEADS - 1, 4)))
                act.activation(pair(ki[0:HD, :]), ps[0:HD], ACT.Copy)
                act.activation(pair(wit[HD:HD + HEADS, :]), ps[HD:HD + HEADS], ACT.Copy)
                for s in range(2):
                    o = 32 * (s ^ 1)
                    got = act.activation(pair(buf[32 * s:32 * s + 32, :]), ps[o:o + 32], ACT.Copy)
                got.then_inc(act_took.mark(use), 1)
                shift_uses.append((rope_made, use))
                next_blocks(use)

            def index_weights(l):
                use = (l, "wT", 0)
                ps = full(use)
                act.activation(widx[:, :, :], ps[:, 0, 0:4 * HEADS].rearrange("p (t x) -> p t x", t=4),
                               ACT.Copy, scale=IDX_W_SCALE).then_inc(act_took.mark(use), 1)

            def index_relu(l, hd):
                for t in MAIN:
                    n = hd * 4 + t - 1
                    use = (l, "idx", hd, t)
                    ps = full(use)
                    if n >= 8:
                        act.wait_ge(score_added.sem, score_added.at((l, hd - 2, t)))
                    if END[t] <= 512:
                        src, dst = ps[:, 0, 0:END[t]], relu[n % 8][:, 0:END[t]]
                    else:
                        src, dst = ps[:, 0:2, 0:END[t] // 2], pair(relu[n % 8][:, 0:END[t]])
                    act.activation(dst, src, ACT.Relu, scale=IDX_SCALE).then_inc(act_took.mark(use), 1)

            def gate_tanh(l, c, half):
                use = (l, "za", c, half)
                a, b = column_halves(META if l else 0)[half]
                act.activation(za[:, c, a:b], full(use)[:, 0, 0:b - a], ACT.Tanh, scale=0.5) \
                    .then_inc(exp_made.mark(use), 1)

            def take_v(l, t):
                use = (l, "v", t)
                ps = full(use)
                act.activation(v[0:SIZE[t], t, :], ps[0:SIZE[t], 0, :], ACT.Copy).then_inc(act_took.mark(use), 1)
                next_blocks(use)

            def exps(l, i):
                t, hd = items[l][i]
                n = SIZE[t]
                act.wait_ge(dve_took.sem, dve_took.at((l, "S", t, hd)))
                act.activation(e[i % 4][0:n, 0:END[t]], e[i % 4][0:n, 0:END[t]], ACT.Exp, scale=-1.0,
                               bias=nmax[0:n, i % 4:i % 4 + 1],
                               accum_out=psums[0:n, i % 4:i % 4 + 1]).then_inc(exp_made.mark((l, i)), 1)

            def take_probs_t(l, i):
                t, hd = items[l][i]
                n = SIZE[t]
                use = (l, "PT", t, hd)
                act.wait_ge(psum_full.sem, psum_full.at(use))
                dst = pt[i % 2]
                if t:
                    act.activation(dst[:, 0:t * P], bank["A"][:, 0, 0:t * P], ACT.Copy)
                act.activation(dst[0:META, SEQ:SEQ + n], bank["B"][0:META, 1, 0:n], ACT.Copy) \
                    .then_inc(act_took.mark(use), 1)

            def y_hi(l, part, t):
                c = 0 if part == "conv" else CT
                j = Y_SLOT[part]
                act.wait_ge(y_made.sem, y_made.at((l, part, t)))
                act.activation(xhi[:, c:c + CT, START[t]:END[t]], yt[j][:, :, 0:SIZE[t]], ACT.Copy) \
                    .then_inc(hi_made.mark((l, part, t)), 1)

            def conv_affine(l, t):
                use = (l, "back", t)
                ps = full(use)
                if t - 2 in query_tiles(l):
                    act.wait_ge(y_made.sem, y_made.at((l, "conv", t - 2)))
                n = SIZE[t]
                for c in range(CT):
                    at = l * CT + c
                    got = act.activation(sl[t % 2][:, c, 0:n], ps[:, 0, c * P:c * P + n], ACT.Identity,
                                         scale=vec[:, V_CLNG + at:V_CLNG + at + 1], bias=vec[:, V_CLNB + at:V_CLNB + at + 1])
                got.then_inc(act_took.mark(use), 1)
                act.wait_ge(act_took.sem, act_took.at(use))
                act.activation(th[t % 2][:, :, 0:n], sl[t % 2][:, :, 0:n], ACT.Tanh, scale=0.5) \
                    .then_inc(exp_made.mark((l, "tanh", t)), 1)

            def x_hi(l, t):
                use = (l, "xT", t)
                ps = full(use)
                n = SIZE[t]
                act.activation(xhi[:, :, START[t]:END[t]],
                               ps[:, :, :].rearrange("p a (k n) -> p (a k) n", n=P)[:, :, 0:n], ACT.Copy) \
                    .then_inc(hi_made.mark((l, "x", t)), 1)

            for c in range(4):
                act.wait_ge(xt0_loaded[c], 16)
                act.activation(xhi[:, 2 * c:2 * c + 2, :], xt0[:, 2 * c:2 * c + 2, :], ACT.Copy) \
                    .then_inc(hi_made.mark((0, "x0", c)), 1)
                if c == 0:
                    act.wait_ge(raw_loaded[0], 16)
                    for half in range(2):
                        a, b = half * BLOCK // 2, (half + 1) * BLOCK // 2
                        act.activation(whi[0][:, a:b], raw[0][:, a:b], ACT.Copy) \
                            .then_inc(hi_made.mark((0, "w0", half)), 1)
            split_hi(1)
            act.wait_ge(consts_loaded, 64)
            act.activation(bmerge[:, :], vec[:, V_BMERGE:V_BSPAT], ACT.Copy, scale=0.5) \
                .then_inc(small_made.mark("bmerge"), 1)
            act.wait_ge(small_made.sem, small_made.at("bmerge"))
            for l in range(DEPTH):
                for c in (0, 2):
                    for name in ("a", "g"):
                        for cc in (c, c + 1):
                            take_channels(l, name, cc)
                            if (l, name, c) == (0, "a", 0):
                                split_hi(2 + cc)
                for c in range(CT):
                    take_channels(l, "qi", c)
                take_index_keys(l)
                for c in range(CT):
                    take_channels(l, "zc", c)
                    if c == 0:
                        index_weights(l)
                    index_relu(l, 2 * c)
                    index_relu(l, 2 * c + 1)
                    next_blocks((l, "zc", c))
                for name in ("q", "k"):
                    for c in range(CT):
                        take_channels(l, name, c)
                for t in TILES:
                    take_v(l, t)
                todo, waiting = extras[l]["act"], []
                n = len(items[l])
                exps(l, 0)
                for i in range(n):
                    if i + 1 < n:
                        exps(l, i + 1)
                    take_probs_t(l, i)
                    for op in todo[i]:
                        if op[0] == "za":
                            gate_tanh(l, *op[1:])
                        elif op[0] == "affine":
                            conv_affine(l, op[1])
                        else:
                            y_hi(l, *op[1:])
                    use = (l, "za", i % CT, i // CT) if i < 8 else (l, "wo", 0, query_tiles(l)[0])
                    if i <= 8:
                        waiting += [(m, half) for m in SPLIT_AT.get(use, []) for half in range(2)]
                    if waiting:
                        split_hi(*waiting.pop(0))
                assert not waiting
                y_hi(l, "attn", 4)
                first = query_tiles(l)[0]
                next_blocks((l, "wo", 1, first))
                for t in query_tiles(l):
                    if l == DEPTH - 1:
                        act.wait_ge(normed.sem, normed.at((l, "h", t)))
                        if t > 1:
                            act.wait_ge(exp_made.sem, exp_made.at((2, "in", t - 1)))
                        act.activation(square[:, :], h[:, t, :], ACT.Square, accum_out=psums[:, t - 1:t]) \
                            .then_inc(exp_made.mark((2, "in", t)), 1)
                        if t > 1:
                            x_hi(l, t - 1)
                    else:
                        x_hi(l, t)
                if l == DEPTH - 1:
                    x_hi(l, 4)

            def take_rows(name, t):
                use = (2, name, t)
                ps = full(use)
                if name == "q":
                    act.activation(qrow[t][:, 0:8, :], ps[:, 0, :].rearrange("p (h d) -> p h d", d=HD), ACT.Copy) \
                        .then_inc(act_took.mark(use), 1)
                elif name == "kv":
                    act.activation(qrow[t][:, 8:10, :], ps[:, 0, 0:P].rearrange("p (h d) -> p h d", d=HD), ACT.Copy)
                    act.activation(v2[:, t, :], ps[:, 0, P:2 * P], ACT.Copy).then_inc(act_took.mark(use), 1)
                elif name == "vin":
                    act.activation(vv[:, t, :], ps[:, 0, :], ACT.Gelu_apprx_tanh).then_inc(act_took.mark(use), 1)
                elif name == "u":
                    act.activation(ug[:, t, :], ps[:, 0, :], ACT.Gelu_apprx_tanh).then_inc(act_took.mark(use), 1)
                else:
                    act.activation(sgb[t][:, :], ps[:, 0, :], ACT.Silu).then_inc(act_took.mark(use), 1)
                next_blocks(use)

            def take_gates(name, c):
                use = (2, name, c)
                ps = full(use)
                if name == "ga":
                    act.activation(sga[:, c, :], ps[:, 0, :], ACT.Silu).then_inc(act_took.mark(use), 1)
                else:
                    if c == 0:
                        act.wait_ge(normed.sem, normed.at((2, "ug", 3)))
                    act.activation(tg[:, c, :], ps[:, 0, :], ACT.Tanh, scale=0.5, bias=bmerge[:, c:c + 1]) \
                        .then_inc(act_took.mark(use), 1)

            def take_qk_t(t):
                use = (2, "qkT", t)
                ps = full(use)
                if t == 0:
                    act.wait_ge(normed.sem, normed.at((2, "rope", 3)))
                for odd in range(2):
                    part = slice(HD * odd, HD * odd + HD)
                    act.activation(q2[t // 2][part, :, t % 2, odd, :],
                                   ps[part, 0, :].rearrange("p (c n) -> p c n", n=P), ACT.Copy)
                for g in range(2):
                    for s in range(2):
                        got = act.activation(k2_hi[HD * s:HD * s + HD, g, P * t:P * t + P],
                                             ps[HD * g:HD * g + HD, 1, 0:P], ACT.Copy)
                got.then_inc(hi_made.mark(use), 1)

            def exps2(i):
                t, hd = items2[i]
                use = (2, "S2", t, hd)
                act.wait_ge(rsum_made.sem, rsum_made.at((2, "max", i)))
                act.activation(e2[i % 3][:, :], psum(use)[:, 0, :], ACT.Exp, bias=nmax[:, i % 4:i % 4 + 1],
                               accum_out=psums[:, i % 4:i % 4 + 1]).then_inc(act_took.mark(use), 1)

            def take_probs2_t(i):
                t, hd = items2[i]
                use = (2, "PT2", t, hd)
                ps = full(use)
                if i >= 2:
                    act.wait_ge(psum_full.sem, psum_full.at((2, "PV2", *items2[i - 2])))
                act.activation(pt2[i % 2][:, :], ps[:, 0, :], ACT.Copy).then_inc(act_took.mark(use), 1)

            def part_hi(part, t):
                c0, c1 = P * t, P * t + P
                if part == "gm":
                    ps = full((2, "gmT", t))
                    act.activation(mlp_hi[:, :, c0:c1], ps[:, 0, :].rearrange("p (c n) -> p c n", n=P), ACT.Copy) \
                        .then_inc(hi_made.mark((2, "gm", t)), 1)
                else:
                    act.wait_ge(y_made.sem, y_made.at((2, "attn", t)))
                    act.activation(attn_hi[:, :, c0:c1], yt2[t % 2][:, :].rearrange("p (c n) -> p c n", n=P), ACT.Copy) \
                        .then_inc(hi_made.mark((2, "attn", t)), 1)

            def y2_hi(d):
                act.wait_ge(y_made.sem, y_made.at((2, "y", d)))
                act.activation(xhi[:, d, 0:SEQ], yt2[d % 2][:, :], ACT.Copy).then_inc(hi_made.mark((2, "y", d)), 1)

            for name in ("q", "kv"):
                for t in range(4):
                    take_rows(name, t)
            for name in ("vin", "u", "gb"):
                for t in range(4):
                    take_rows(name, t)
                    if name == "u":
                        take_qk_t(t)
            for c in range(CT):
                take_gates("ga", c)
                next_blocks((2, "ga", c))
            n, waiting = len(items2), []
            exps2(0)
            for i in range(n):
                if i + 1 < n:
                    exps2(i + 1)
                if i % 2 and i < 8:
                    part_hi("gm", i // 2)
                take_probs2_t(i)
                if i % 2 == 0:
                    take_gates("gm", i // 2)
                    waiting += [(m, half) for m in SPLIT_AT.get((2, "gm", i // 2), []) for half in range(2)]
                if i > 1 and i % HEADS == 1:
                    part_hi("attn", i // HEADS - 1)
                if waiting:
                    split_hi(*waiting.pop(0))
            assert not waiting
            part_hi("attn", 3)
            next_blocks((2, "yb", 0))
            for d in range(KD):
                if d == 4:
                    next_blocks((2, "ya", 3))
                    next_blocks((2, "yb", 4))
                y2_hi(d)
            next_blocks((2, "ya", 7))
            next_blocks((2, "wo", 0, 0))
            for t in range(4):
                act.wait_ge(dve_took.sem, dve_took.at((2, "wo", 1, t)))
                act.activation(tg[:, 2 * t:2 * t + 2, :], h[:, t + 1, :].rearrange("p (a b) -> p a b", a=2), ACT.Square,
                               accum_out=psums[:, t:t + 1]).then_inc(exp_made.mark(("out", t)), 1)

        @block.gpsimd
        def _(pool):
            def split_lo(n):
                width = BLOCKS[n][1]
                pool.wait_ge(weights_hi.sem, weights_hi.at(n))
                cut = [0, width // 2, width]
                for a, b in zip(cut, cut[1:]):
                    got = pool.tensor_tensor(wlo[n % RING][:, a:b], raw[n % RING][:, a:b],
                                             whi[n % RING][:, a:b].bitcast(F32), ALU.subtract)
                got.then_inc(weights_lo.mark(n), 1)

            def next_blocks(use):
                for n in SPLIT_AT.get(use, []):
                    split_lo(n)

            shifts = [0]

            def times_sin(l, name, c):
                use = (l, name, c)
                first = META if l and name in ("q", "qi") else 0
                rows = HD if name == "ki" else P
                buf = xs[shifts[0] % 4]
                shifts[0] += 1
                pool.wait_ge(act_took.sem, act_took.at(use))
                pool.tensor_tensor(buf[0:rows, first:L], buf[0:rows, first:L], sin[0:rows, first:L], ALU.mult) \
                    .then_inc(rope_sin.mark(use), 1)

            def reciprocal_deviation(step, src, n, rows, slot, scale, eps):
                pool.tensor_scalar(veps[0:rows, slot:slot + n], src, scale, eps, ALU.mult, ALU.add) \
                    .then_inc(pool_step.mark(step), 1)
                pool.wait_ge(pool_step.sem, pool_step.at(step))
                pool.tensor_tensor(rstd[0:rows, slot:slot + n], veps[0:rows, slot:slot + n],
                                   minus_half[0:rows, 0:n], ALU.pow).then_inc(rstd_made.mark(step), 1)

            def part_low(l, part, t):
                n = SIZE[t]
                c = 0 if part == "conv" else CT
                pool.wait_ge(hi_made.sem, hi_made.at((l, part, t)))
                pool.tensor_tensor(xlo[:, c:c + CT, START[t]:END[t]], yt[Y_SLOT[part]][:, :, 0:n],
                                   xhi[:, c:c + CT, START[t]:END[t]].bitcast(F32), ALU.subtract) \
                    .then_inc(part_lo.mark((l, part, t)), 1)

            def ln_deviation(step, t, rows):
                pool.wait_ge(stats_made.sem, stats_made.at(step))
                reciprocal_deviation(step, meanvar[0:rows, t, 1:2], 1, rows, t, 1.0, LN_EPS)

            pool.memset(u[:, :, 0:PAD], 0.0).then_inc(set_up.mark("pad"), 1)
            pool.memset(minus_half[:, :], -0.5).then_inc(set_up.mark("half"), 1)
            pool.memset(mask[0:META, MASK0_AT:MASK0_AT + META], 0.0).then_inc(set_up.mark("mask"), 1)
            pool.wait_ge(set_up.sem, set_up.at("mask"))
            pool.affine_select(out=mask[0:META, MASK0_AT:MASK0_AT + META],
                               in_=mask[0:META, MASK0_AT:MASK0_AT + META], compare_op=ALU.is_ge, fill=HIDE,
                               base=0, pattern=[[-1, META]], channel_multiplier=1) \
                .then_inc(set_up.mark("mask0"), 1)
            for n in range(1, RING):
                split_lo(n)
            pool.wait_ge(consts_loaded, 64)
            for l in range(DEPTH):
                for c in (0, 2):
                    for name in ("a", "g"):
                        next_blocks((l, name, c))
                        next_blocks((l, name, c + 1))
                shifts[0] += 4
                for c in range(CT):
                    times_sin(l, "qi", c)
                    next_blocks((l, "qi", c))
                times_sin(l, "ki", 0)
                next_blocks((l, "ki", 0))
                for c in range(CT):
                    next_blocks((l, "zc", c))
                for t in MAIN:
                    a = SCORE_AT[t] + START[t]
                    pool.wait_ge(score_added.sem, score_added.at((l, HEADS - 1, t)))
                    pool.affine_select(out=score[:, a:a + P], in_=score[:, a:a + P], compare_op=ALU.is_ge,
                                       fill=FILL, base=0, pattern=[[-1, P]], channel_multiplier=1) \
                        .then_inc(causal_done.mark((l, "score", t)), 1)
                for name in ("q", "k"):
                    for c in range(CT):
                        times_sin(l, name, c)
                        next_blocks((l, name, c))
                for t in TILES:
                    next_blocks((l, "v", t))
                for t in MAIN:
                    a = SCORE_AT[t] + START[t]
                    pool.wait_ge(mask_made.sem, mask_made.at((l, t)))
                    pool.affine_select(out=mask[:, a:a + P], in_=mask[:, a:a + P], compare_op=ALU.is_ge,
                                       fill=HIDE, base=0, pattern=[[-1, P]], channel_multiplier=1) \
                        .then_inc(causal_done.mark((l, "mask", t)), 1)
                waiting = []
                for use in USES[USES.index((l, "za", 0, 0)):USES.index((l, "wo", 0, query_tiles(l)[0])) + 1]:
                    waiting += SPLIT_AT.get(use, [])
                for _ in range(2):
                    split_lo(waiting.pop(0))
                for ops in extras[l]["pool"]:
                    for op in ops:
                        if op[0] == "deviation":
                            ln_deviation((l, "conv", op[1]), op[1], SIZE[op[1]])
                        else:
                            part_low(l, *op[1:])
                part_low(l, "attn", 4)
                for m in waiting:
                    split_lo(m)
                first = query_tiles(l)[0]
                waiting = list(SPLIT_AT[(l, "wo", 1, first)])
                for t in query_tiles(l):
                    ln_deviation((l, "post", t), t, SIZE[t])
                    if waiting:
                        split_lo(waiting.pop(0))
                    if l == DEPTH - 1:
                        pool.wait_ge(exp_made.sem, exp_made.at((2, "in", t)))
                        reciprocal_deviation((2, "in", t), psums[:, t - 1:t], 1, P, 8 + t, 1.0 / D, EPS)
            def unit_scale(name, t):
                h0, h1 = (0, HEADS) if name == "q" else (HEADS, HEADS + 2)
                step = (2, name, t)
                pool.wait_ge(stats_made.sem, stats_made.at(step))
                pool.tensor_scalar(squares[:, t, h0:h1], squares[:, t, h0:h1], 1.0 / HD, EPS, ALU.mult, ALU.add) \
                    .then_inc(pool_step.mark(step), 1)
                pool.wait_ge(pool_step.sem, pool_step.at(step))
                pool.tensor_tensor(unit[:, t, h0:h1], squares[:, t, h0:h1], minus_half[:, h0:h1], ALU.pow) \
                    .then_inc(rstd_made.mark(step), 1)

            for t in range(4):
                next_blocks((2, "q", t))
                unit_scale("q", t)
            for t in range(4):
                next_blocks((2, "kv", t))
                unit_scale("k", t)
            for t in range(4):
                next_blocks((2, "vin", t))
            for t in range(4):
                pool.wait_ge(stats_made.sem, stats_made.at((2, "v", t)))
                reciprocal_deviation((2, "v", t), meanvar[:, t, 1:2], 1, P, 12 + t, 1.0, EPS)
            for name in ("u", "gb", "ga"):
                for t in range(4):
                    next_blocks((2, name, t))
            for c in range(2 * KD):
                next_blocks((2, "gm", c))
            for d in range(KD):
                next_blocks((2, "yb", d))
                next_blocks((2, "ya", d))
            next_blocks((2, "wo", 0, 0))
            for t in range(4):
                pool.wait_ge(exp_made.sem, exp_made.at(("out", t)))
                reciprocal_deviation(("out", t), psums[:, t:t + 1], 1, P, t, 1.0 / D, EPS)

        @block.tensor
        def _(pe):
            last_use = {}
            turn = {"AB": 0, "CD": 0}
            index_buf = [None]

            def claim(use, buf, banks=(0, 1)):
                before = {last_use[buf, b] for b in banks if (buf, b) in last_use}
                for prev in sorted(before, key=str):
                    pe.wait_ge(*taken(prev))
                for b in banks:
                    last_use[buf, b] = use
                psum_of.setdefault(use, (buf, banks[0]))
                return bank[buf][:, banks[0]:banks[-1] + 1, :]

            def next_buf(kind):
                turn[kind] += 1
                return kind[turn[kind] % 2]

            def weights(n):
                if n:
                    pe.wait_ge(weights_lo.sem, weights_lo.at(n))
                return whi[n % RING], wlo[n % RING]

            x = (xhi, xlo)

            def channel_weights(l, name, c):
                if name == "ki":
                    n, width, cols, at = NUMBER[(l, "ki", 0)], HD + HEADS, HD + HEADS, 0
                else:
                    n, width, cols, at = NUMBER[(l, name, c - c % 2)], 2 * P, P, c % 2 * P
                w = [part[:, 0:KD * width].rearrange("p (k c) -> p k c", k=KD) for part in weights(n)]
                return w, cols, at

            def product(ps, w, cols, at, pieces, waits=None):
                for kt in range(KD):
                    if waits:
                        waits(kt)
                    for wp, xp in PASSES:
                        for i, a, b in pieces:
                            mm = pe.matmul(ps[0:cols, i, 0:b - a], w[wp][:, kt, at:at + cols], x[xp][:, kt, a:b],
                                           start=(kt == 0 and wp + xp == 0), stop=(kt == KD - 1 and wp == 1))
                return mm

            def pieces_of(l, name):
                (a, m), (_, b) = column_halves(META if l and name in ("zc", "za", "q", "qi") else 0)
                return (0, a, m), (1, m, b)

            def channels(l, name, c, waits=None, buf=None):
                use = (l, name, c)
                w, cols, at = channel_weights(l, name, c)
                pieces = ((0, META, L),) if l == 2 else pieces_of(l, name)
                ps = claim(use, buf or next_buf("AB"))
                product(ps, w, cols, at, pieces, waits).then_inc(psum_full.mark(use), 1)

            def gate_half(l, c, half):
                use = (l, "za", c, half)
                w, cols, at = channel_weights(l, "za", c)
                _, a, b = pieces_of(l, "za")[half]
                ps = claim(use, "AD"[c % 2], (1,))
                product(ps, w, cols, at, ((0, a, b),)).then_inc(psum_full.mark(use), 1)

            def rows(use, first_block, act_parts, c0, n_blocks, width=DC, at=0, kts=4, waits=None, buf=None):
                ps = claim(use, buf or next_buf("AB"))
                for half in range(n_blocks):
                    w = [part[:, :].rearrange("p (k c) -> p k c", k=kts) for part in weights(first_block + half)]
                    for kk in range(kts):
                        kt = half * kts + kk
                        if waits:
                            waits(kt)
                        for wp, xp in PASSES:
                            mm = pe.matmul(ps[:, 0, 0:width], act_parts[xp][:, kt, c0:c0 + P], w[wp][:, kk, at:at + width],
                                           start=(kt == 0 and wp + xp == 0), stop=(kt == KD - 1 and wp == 1))
                mm.then_inc(psum_full.mark(use), 1)

            def index_weights(l):
                use = (l, "wT", 0)
                ps = claim(use, next_buf("CD"))
                pe.wait_ge(act_took.sem, act_took.at((l, "ki", 0)))
                for t in MAIN:
                    mm = pe.transpose(ps[:, 0, (t - 1) * HEADS:t * HEADS], wit[HD:HD + HEADS, START[t]:END[t]],
                                      ident[HD:HD + HEADS, HD:HD + HEADS])
                mm.then_inc(psum_full.mark(use), 1)

            def logits(use, ps, qs, ks, hd, t, n_keys):
                s = HD * (hd % 2)
                lhs = qs[s:s + HD, hd // 2, START[t]:END[t]]
                if n_keys <= 512:
                    pieces = ((0, n_keys),)
                else:
                    pieces = ((0, n_keys // 2), (n_keys // 2, n_keys))
                for i, (a, b) in enumerate(pieces):
                    mm = pe.matmul(ps[0:SIZE[t], i, 0:b - a], lhs, ks[s:s + HD, a:b], start=True, stop=True)
                mm.then_inc(psum_full.mark(use), 1)

            def index_scores(l, hd):
                pe.wait_ge(rope_made.sem, rope_made.at((l, "ki", "copy")))
                pe.wait_ge(rope_made.sem, rope_made.at((l, "qi", hd // 2)))
                for t in MAIN:
                    use = (l, "idx", hd, t)
                    if t < 4:
                        n = hd * 3 + t - 1
                        ps = claim(use, (index_buf[0], "C")[n // 2 % 2], (n % 2,))
                    else:
                        ps = claim(use, "D")
                    logits(use, ps, qi, ki, hd, t, END[t])

            def attention_logits(l, i):
                t, hd = items[l][i]
                use = (l, "S", t, hd)
                logits(use, claim(use, next_buf("CD"), (0,) if t < 4 else (0, 1)), q, k[:, hd // 2, :], hd, t, END[t])

            def turn_probs(l, i):
                t, hd = items[l][i]
                n = SIZE[t]
                use = (l, "PT", t, hd)
                main, meta = claim(use, "A", (0,)), claim(use, "B", (1,))
                pe.wait_ge(probs_made.sem, probs_made.at((l, i)))
                src = e[i % 4]
                for j in range(1, t + 1):
                    pe.transpose(main[:, 0, (j - 1) * P:(j - 1) * P + n], src[0:n, START[j]:END[j]], ident[0:n, 0:n])
                pe.transpose(meta[0:META, 0, 0:n], src[0:n, 0:META], ident[0:n, 0:n]) \
                    .then_inc(psum_full.mark(use), 1)

            def probs_times_v(l, i):
                t, hd = items[l][i]
                n = SIZE[t]
                use = (l, "O", t)
                ps = claim(use, "B", (0,)) if hd == 0 else bank["B"]
                pe.wait_ge(act_took.sem, act_took.at((l, "PT", t, hd)))
                s = HD * (hd % 2)
                out = ps[s:s + HD, 0, hd // 2 * P:hd // 2 * P + n]
                src = pt[i % 2]
                mm = pe.matmul(out, v[0:META, 0, hd * HD:hd * HD + HD], src[0:META, SEQ:SEQ + n],
                               start=True, stop=(t == 0))
                for j in range(1, t + 1):
                    mm = pe.matmul(out, v[:, j, hd * HD:hd * HD + HD], src[:, (j - 1) * P:(j - 1) * P + n],
                                   start=False, stop=(j == t))
                if hd == HEADS - 1:
                    mm.then_inc(psum_full.mark(use), 1)

            def turn_conv(l, t):
                use = (l, "fwd", t)
                ps = claim(use, "A" if t == 4 else "D", (1,))
                n = SIZE[t]
                for c in range(CT):
                    pe.wait_ge(tap_done.sem, tap_done.at((l, c, TAPS - 1)))
                    mm = pe.transpose(ps[0:n, 0, c * P:c * P + P], acc[:, c, START[t]:END[t]], ident[:, :])
                mm.then_inc(psum_full.mark(use), 1)

            def turn_conv_back(l, t):
                use = (l, "back", t)
                ps = claim(use, "A", (1,))
                n = SIZE[t]
                pe.wait_ge(dve_took.sem, dve_took.at((l, "fwd", t)))
                for c in range(CT):
                    mm = pe.transpose(ps[:, 0, c * P:c * P + n], cnorm[t][0:n, c * P:c * P + P], ident[0:n, 0:n])
                mm.then_inc(psum_full.mark(use), 1)

            def turn_rows(l, t):
                use = (l, "xT", t)
                ps = claim(use, next_buf("CD"))
                n = SIZE[t]
                pe.wait_ge(normed.sem, normed.at((l, "x", t)))
                src = h[0:n, t, :] if l == 0 else hn[t % 2][0:n, :]
                for kt in range(KD):
                    mm = pe.transpose(ps[:, kt // 4, kt % 4 * P:kt % 4 * P + n], src[:, kt * P:kt * P + P], ident[0:n, 0:n])
                mm.then_inc(psum_full.mark(use), 1)

            def output_rows(l, half, t, buf=None):
                if half == 0:
                    pe.wait_ge(part_lo.sem, part_lo.at((l, "conv", t)))
                    pe.wait_ge(part_lo.sem, part_lo.at((l, "attn", t)))
                rows((l, "wo", half, t), NUMBER[(l, "wo", half, 0)], x, START[t], 2, buf=buf)

            def x_ready(l, t):
                pe.wait_ge(dve_took.sem, dve_took.at((l, "xT", t)))

            for l in range(DEPTH):
                if l == 0:
                    def first_x(kt):
                        if kt % 2 == 0:
                            pe.wait_ge(lo_made.sem, lo_made.at((0, "x0", kt // 2)))
                        if kt % 4 == 0:
                            pe.wait_ge(lo_made.sem, lo_made.at((0, "w0", kt // 4)))

                    channels(0, "a", 0, first_x)
                    channels(0, "a", 1)
                    channels(0, "g", 0)
                else:
                    started = []
                    for t in (0, 1, 2):
                        x_ready(l - 1, t)
                    for name, c, turned in (("a", 0, 3), ("a", 1, 4), ("g", 0, None)):
                        use = (l, name, c)
                        ps = claim(use, next_buf("CD" if name == "g" else "AB"))
                        w, cols, at = channel_weights(l, name, c)
                        first, second = pieces_of(l, name)
                        assert first[2] <= END[2]
                        product(ps, w, cols, at, (first,))
                        started.append((use, ps, w, cols, at, second))
                        if turned:
                            turn_rows(l - 1, turned)
                    x_ready(l - 1, 3)
                    x_ready(l - 1, 4)
                    for use, ps, w, cols, at, second in started:
                        product(ps, w, cols, at, (second,)).then_inc(psum_full.mark(use), 1)
                channels(l, "g", 1)
                for name in ("a", "g"):
                    for c in (2, 3):
                        channels(l, name, c)
                for c in range(CT):
                    channels(l, "qi", c)
                channels(l, "ki", 0)
                zc_buf, index_buf[0] = next_buf("AB"), "AB"[(turn["AB"] + 1) % 2]
                for c in range(CT):
                    channels(l, "zc", c, buf=zc_buf)
                    if c == 0:
                        index_weights(l)
                    index_scores(l, 2 * c)
                    index_scores(l, 2 * c + 1)
                for name in ("q", "k"):
                    for c in range(CT):
                        channels(l, name, c)
                for t in TILES:
                    rows((l, "v", t), NUMBER[(l, "v", 0)], x, START[t], 2)
                todo = extras[l]["pe"]
                n = len(items[l])
                for c in range(CT):
                    pe.wait_ge(rope_made.sem, rope_made.at((l, "q", c)))
                    pe.wait_ge(rope_made.sem, rope_made.at((l, "k", c)))
                for i in range(3):
                    attention_logits(l, i)
                for i in range(n):
                    if i + 3 < n:
                        attention_logits(l, i + 3)
                    for op in todo[i]:
                        if op[0] == "za":
                            gate_half(l, *op[1:])
                        elif op[0] == "fwd":
                            turn_conv(l, op[1])
                        else:
                            turn_conv_back(l, op[1])
                    if i == n - 2:
                        output_rows(l, 0, query_tiles(l)[0], "C")
                    turn_probs(l, i)
                    if i:
                        probs_times_v(l, i - 1)
                probs_times_v(l, n - 1)
                tiles = list(query_tiles(l))
                turn["AB"] = 1
                for half in range(2):
                    for t in tiles:
                        if (half, t) != (0, tiles[0]):
                            output_rows(l, half, t)
                        if half == 1 and t - 2 in tiles:
                            turn_rows(l, t - 2)

            SPARE = "B", (1,)

            def merge_gate(c):
                use = (2, "gm", c)
                w, cols, at = channel_weights(2, "gm", c)
                ps = claim(use, *SPARE)
                product(ps, w, cols, at, ((0, META, L),)).then_inc(psum_full.mark(use), 1)

            def turn_qk(t):
                use = (2, "qkT", t)
                ps = claim(use, next_buf("CD"))
                pe.wait_ge(normed.sem, normed.at((2, "rope", t)))
                src = qrot[t][:, :, :].rearrange("p h d -> p (h d)")
                for c in range(5):
                    mm = pe.transpose(ps[:, c // 4, c % 4 * P:c % 4 * P + P], src[:, c * P:c * P + P], ident[:, :])
                mm.then_inc(psum_full.mark(use), 1)

            def mix_positions(pair_):
                use = (2, "vmix", pair_)
                ps = claim(use, next_buf("CD"))
                for t in range(4):
                    pe.wait_ge(normed.sem, normed.at((2, "v", t)))
                pe.wait_ge(block2_loaded, 8 * 16)
                for i in range(2):
                    g = 2 * pair_ + i
                    mm = pe.matmul(ps[:, i, 0:4 * GD], wst[:, g, :], vv[:, :, g * GD:g * GD + GD], start=True, stop=True)
                mm.then_inc(psum_full.mark(use), 1)

            def turn_mlp(t):
                use = (2, "gmT", t)
                ps = claim(use, *SPARE)
                for pair_ in range(4):
                    pe.wait_ge(dve_took.sem, dve_took.at((2, "vmix", pair_)))
                for c in range(CT):
                    mm = pe.transpose(ps[:, 0, c * P:c * P + P], ug[:, t, c * P:c * P + P], ident[:, :])
                mm.then_inc(psum_full.mark(use), 1)

            def logits2(i):
                t, hd = items2[i]
                use = (2, "S2", t, hd)
                ps = claim(use, "CD"[i // 2 % 2], (i % 2,))
                rows_ = q2[t // 2][:, hd // 2, t % 2, hd % 2, :]
                pe.matmul(ps[:, 0, :], rows_, k2_hi[:, hd // 4, :], start=True, stop=False)
                pe.matmul(ps[:, 0, :], rows_, k2_lo[:, hd // 4, :], start=False, stop=True) \
                    .then_inc(psum_full.mark(use), 1)

            def turn_probs2(i):
                t, hd = items2[i]
                use = (2, "PT2", t, hd)
                ps = claim(use, "A", (i % 2,))
                pe.wait_ge(probs_made.sem, probs_made.at((2, i)))
                for j in range(4):
                    mm = pe.transpose(ps[:, 0, j * P:j * P + P], e2[i % 3][:, j * P:j * P + P], ident[:, :])
                mm.then_inc(psum_full.mark(use), 1)

            def probs_times_v2(i):
                t, hd = items2[i]
                ps = claim((2, "O2", t), "B", (0,)) if hd == 0 else bank["B"]
                pe.wait_ge(act_took.sem, act_took.at((2, "PT2", t, hd)))
                s, g = HD * (hd % 2), hd // 4
                for j in range(4):
                    mm = pe.matmul(ps[s:s + HD, 0, hd // 2 * P:hd // 2 * P + P], v2[:, j, g * HD:g * HD + HD],
                                   pt2[i % 2][:, j * P:j * P + P], start=(j == 0), stop=(j == 3))
                mm.then_inc(psum_full.mark((2, "PV2", t, hd)), 1)

            def branch(name, d, buf=None):
                use = (2, name, d)
                n = NUMBER[(2, name, d - d % 4)]
                w = [part[:, :].rearrange("p (k c) -> p k c", k=CT) for part in weights(n)]
                parts = (attn_hi, attn_lo) if name == "ya" else (mlp_hi, mlp_lo)
                ps = claim(use, buf or next_buf("AB"))
                for kt in range(CT):
                    for wp, xp in PASSES:
                        mm = pe.matmul(ps[:, 0, :], w[wp][:, kt, d % 4 * P:d % 4 * P + P], parts[xp][:, kt, :],
                                       start=(kt == 0 and wp + xp == 0), stop=(kt == CT - 1 and wp == 1))
                mm.then_inc(psum_full.mark(use), 1)

            for t in range(4):
                x_ready(1, t + 1)
                rows((2, "q", t), NUMBER[(2, "q", 0)], x, META + P * t, 2)
                if t < 2:
                    turn_rows(1, t + 3)
            for t in range(4):
                rows((2, "kv", t), NUMBER[(2, "kv", 0)], x, META + P * t, 1, 2 * P, 0, KD)
            for name in ("vin", "u", "gb"):
                for t in range(4):
                    rows((2, name, t), NUMBER[(2, name, 0)], x, META + P * t, 2)
                    if name == "u":
                        turn_qk(t)
            turn["CD"] = 1
            for c in range(CT):
                channels(2, "ga", c)
                mix_positions(c)
            n = len(items2)
            for i in range(3):
                logits2(i)
            for i in range(n):
                if i + 3 < n:
                    logits2(i + 3)
                if i % 2 == 0:
                    merge_gate(i // 2)
                if i % 2 and i < 8:
                    turn_mlp(i // 2)
                turn_probs2(i)
                if i:
                    probs_times_v2(i - 1)
            probs_times_v2(n - 1)
            for t in range(4):
                pe.wait_ge(dve_took.sem, dve_took.at((2, "gmT", t)))
            for d in range(KD):
                branch("yb", d, None if d else "C")
                if d == 0:
                    for t in range(4):
                        pe.wait_ge(lo_made.sem, lo_made.at((2, "attn", t)))
                branch("ya", d)
            for half in range(2):
                for t in range(4):
                    def merged(kt):
                        pe.wait_ge(lo_made.sem, lo_made.at((2, "y", kt)))

                    rows((2, "wo", half, t), NUMBER[(2, "wo", half, 0)], x, P * t, 2,
                         waits=merged if half + t == 0 else None)

        @block.vector
        def _(dve):
            def full(use):
                dve.wait_ge(psum_full.sem, psum_full.at(use))
                return psum(use)

            def pair(ap):
                return ap.rearrange("p (a b) -> p a b", a=2)

            shifts = [0]

            def gate_conv_input(l, c):
                buf = xs[shifts[0] % 4]
                shifts[0] += 1
                dve.wait_ge(act_took.sem, act_took.at((l, "g", c)))
                dve.scalar_tensor_tensor(u[:, c, PAD:PAD + L], buf[:, :], 1.0, u[:, c, PAD:PAD + L],
                                         ALU.add, ALU.mult).then_inc(u_made.mark((l, c)), 1)

            def conv(l, c, first, last):
                x0 = META if l else 0
                for tap in range(first, last):
                    for cc in (c, c + 1):
                        w = vec[:, V_CONVW + (l * TAPS + tap) * CT + cc:V_CONVW + (l * TAPS + tap) * CT + cc + 1]
                        src = u[:, cc, tap + x0:tap + L]
                        dst = acc[:, cc, x0:L]
                        if tap == 0:
                            dve.wait_ge(u_made.sem, u_made.at((l, cc)))
                            b = vec[:, V_CONVB + l * CT + cc:V_CONVB + l * CT + cc + 1]
                            got = dve.tensor_scalar(dst, src, w, b, ALU.mult, ALU.add)
                        else:
                            dve.wait_ge(tap_done.sem, tap_done.at((l, cc, tap - 1)))
                            got = dve.scalar_tensor_tensor(dst, src, w, dst, ALU.mult, ALU.add)
                        got.then_inc(tap_done.mark((l, cc, tap)), 1)

            def rope(l, name, c):
                use = (l, name, c)
                first = META if l and name in ("q", "qi") else 0
                n = HD if name == "ki" else P
                buf = xs[shifts[0] % 4]
                shifts[0] += 1
                dst = ki[0:n, :] if name == "ki" else {"qi": qi, "q": q, "k": k}[name][:, c, first:L]
                dve.wait_ge(act_took.sem, act_took.at(use))
                dve.tensor_tensor(dst, dst, cos[0:n, first:L], ALU.mult).then_inc(rope_cos.mark(use), 1)
                dve.wait_ge(rope_cos.sem, rope_cos.at(use))
                dve.wait_ge(rope_sin.sem, rope_sin.at(use))
                dve.tensor_tensor(dst, dst, buf[0:n, first:L], ALU.add).then_inc(rope_made.mark(use), 1)
                if name == "ki":
                    dve.wait_ge(rope_made.sem, rope_made.at(use))
                    dve.tensor_copy(ki[HD:P, :], ki[0:HD, :]).then_inc(rope_made.mark((l, "ki", "copy")), 1)

            def add_scores(l, hd):
                if hd == 0:
                    dve.wait_ge(act_took.sem, act_took.at((l, "wT", 0)))
                for t in MAIN:
                    dve.wait_ge(act_took.sem, act_took.at((l, "idx", hd, t)))
                    dst = score[:, SCORE_AT[t]:SCORE_AT[t] + END[t]]
                    src = relu[(hd * 4 + t - 1) % 8][:, 0:END[t]]
                    w = widx[:, t - 1, hd:hd + 1]
                    if hd == 0:
                        got = dve.tensor_scalar(dst, src, w, 0.0, ALU.mult, ALU.add)
                    else:
                        dve.wait_ge(score_added.sem, score_added.at((l, hd - 1, t)))
                        got = dve.scalar_tensor_tensor(dst, src, w, dst, ALU.mult, ALU.add)
                    got.then_inc(score_added.mark((l, hd, t)), 1)

            def topk(l, between):
                rounds = -(-TOPK // 8)
                for r in range(rounds):
                    for t in MAIN:
                        vals = score[:, SCORE_AT[t]:SCORE_AT[t] + END[t]]
                        if r == 0:
                            dve.wait_ge(causal_done.sem, causal_done.at((l, "score", t)))
                        else:
                            dve.wait_ge(topk_marked.sem, topk_marked.at((l, r - 1, t)))
                        dve.max(top8[:, t - 1, :], vals).then_inc(topk_max.mark((l, r, t)), 1)
                    if r == rounds - 1:
                        dve.wait_ge(topk_max.sem, topk_max.at((l, r, 4)))
                        dve.memset(top8[:, :, TOPK - 8 * r:8], MARK).then_inc(topk_max.mark((l, "cut")), 1)
                        dve.wait_ge(topk_max.sem, topk_max.at((l, "cut")))
                    for t in MAIN:
                        vals = score[:, SCORE_AT[t]:SCORE_AT[t] + END[t]]
                        dve.wait_ge(topk_max.sem, topk_max.at((l, r, t)))
                        dve.match_replace(vals, top8[:, t - 1, :], vals, MARK).then_inc(topk_marked.mark((l, r, t)), 1)
                    between(r)
                for t in MAIN:
                    a, b = SCORE_AT[t], SCORE_AT[t] + END[t]
                    dve.wait_ge(topk_marked.sem, topk_marked.at((l, rounds - 1, t)))
                    dve.tensor_scalar(mask[:, a:b], score[:, a:b], MARK, HIDE, ALU.not_equal, ALU.mult) \
                        .then_inc(mask_made.mark((l, t)), 1)

            def conv_stats(l, t):
                ps = full((l, "fwd", t))
                n = SIZE[t]
                step = (l, "conv", t)
                dve.bn_stats(stats[0:n, t, 0, :], ps[0:n, 0, :]).then_inc(dve_step.mark(step), 1)
                dve.wait_ge(dve_step.sem, dve_step.at(step))
                dve.bn_aggr(meanvar[0:n, t, :], stats[0:n, t, 0, :]).then_inc(stats_made.mark(step), 1)

            def conv_norm(l, t):
                use = (l, "fwd", t)
                n = SIZE[t]
                dve.wait_ge(stats_made.sem, stats_made.at((l, "conv", t)))
                dve.wait_ge(rstd_made.sem, rstd_made.at((l, "conv", t)))
                dve.tensor_scalar(cnorm[t][0:n, :], psum(use)[0:n, 0, :], meanvar[0:n, t, 0:1], rstd[0:n, t:t + 1],
                                  ALU.subtract, ALU.mult).then_inc(dve_took.mark(use), 1)

            def masked_logits(l, i):
                t, hd = items[l][i]
                n = SIZE[t]
                use = (l, "S", t, hd)
                ps = full(use)
                if hd == 0 and t:
                    dve.wait_ge(causal_done.sem, causal_done.at((l, "mask", t)))
                if i >= 4:
                    dve.wait_ge(psum_full.sem, psum_full.at((l, "PT", *items[l][i - 4])))
                a = SCORE_AT[t] if t else MASK0_AT
                m = mask[0:n, a:a + END[t]]
                dst = e[i % 4][0:n, 0:END[t]]
                if END[t] <= 512:
                    src = ps[0:n, 0, 0:END[t]]
                else:
                    src, m, dst = ps[0:n, 0:2, 0:END[t] // 2], pair(m), pair(dst)
                dve.tensor_tensor_reduce(dst, src, m, -SCALE, 3.0e38, ALU.add, ALU.min,
                                         nmax[0:n, i % 4:i % 4 + 1]).then_inc(dve_took.mark(use), 1)

            def normalise(l, i):
                t, hd = items[l][i]
                n = SIZE[t]
                dve.wait_ge(exp_made.sem, exp_made.at((l, i)))
                dve.reciprocal(rsums[0:n, i % 4:i % 4 + 1], psums[0:n, i % 4:i % 4 + 1]).then_inc(rsum_made.mark((l, i)), 1)
                dve.wait_ge(rsum_made.sem, rsum_made.at((l, i)))
                dve.tensor_scalar(e[i % 4][0:n, 0:END[t]], e[i % 4][0:n, 0:END[t]], rsums[0:n, i % 4:i % 4 + 1], None,
                                  ALU.mult).then_inc(probs_made.mark((l, i)), 1)

            y_parts = {}

            def gate(l, c, half):
                use = (l, "za", c, half)
                a, b = column_halves(META if l else 0)[half]
                dst = za[:, c, a:b]
                dve.wait_ge(exp_made.sem, exp_made.at(use))
                dve.scalar_tensor_tensor(dst, dst, 1.0, psum(use)[:, 0, 0:b - a], ALU.add, ALU.mult) \
                    .then_inc(dve_took.mark(use), 1)

            def y_part(l, part, t):
                n = SIZE[t]
                j = Y_SLOT[part]
                if j in y_parts:
                    dve.wait_ge(part_lo.sem, part_lo.at(y_parts[j]))
                y_parts[j] = (l, part, t)
                dst = yt[j][:, :, 0:n]
                if part == "attn":
                    use = (l, "O", t)
                    ps = full(use)
                    _, middle = column_halves(META if l else 0)[0]
                    dve.wait_ge(dve_took.sem, dve_took.at((l, "za", CT - 1, 0 if END[t] <= middle else 1)))
                    dve.scalar_tensor_tensor(dst, ps[:, 0, :].rearrange("p (c n) -> p c n", n=P)[:, :, 0:n], 0.5,
                                             za[:, :, START[t]:END[t]], ALU.mult, ALU.mult) \
                        .then_inc(y_made.mark((l, part, t)), 1)
                else:
                    z = sl[t % 2][:, :, 0:n]
                    dve.wait_ge(exp_made.sem, exp_made.at((l, "tanh", t)))
                    dve.scalar_tensor_tensor(z, th[t % 2][:, :, 0:n], 1.0, z, ALU.add, ALU.mult) \
                        .then_inc(dve_step.mark((l, "silu", t)), 1)
                    dve.wait_ge(dve_step.sem, dve_step.at((l, "silu", t)))
                    dve.scalar_tensor_tensor(dst, z, 0.5, zc[:, :, START[t]:END[t]], ALU.mult, ALU.mult) \
                        .then_inc(y_made.mark((l, part, t)), 1)

            def residual(l, half, t):
                use = (l, "wo", half, t)
                n = SIZE[t]
                ps = full(use)
                if l == 0 and half == 0:
                    dve.wait_ge(h_loaded, 32)
                dst = h[0:n, t, half * 512:half * 512 + 512]
                dve.scalar_tensor_tensor(dst, dst, ALPHA, ps[0:n, 0, :], ALU.mult, ALU.add) \
                    .then_inc(dve_took.mark(use), 1)
                dve.wait_ge(dve_took.sem, dve_took.at(use))
                dve.bn_stats(stats[0:n, t, half, :], dst).then_inc(dve_step.mark((l, "post", half, t)), 1)

            def post_norm(l, t):
                n = SIZE[t]
                step = (l, "post", t)
                row = h[0:n, t, :]
                dve.wait_ge(dve_step.sem, dve_step.at((l, "post", 1, t)))
                dve.bn_aggr(meanvar[0:n, t, :], stats[0:n, t, :, :].rearrange("p a b -> p (a b)")) \
                    .then_inc(stats_made.mark(step), 1)
                dve.wait_ge(stats_made.sem, stats_made.at(step))
                dve.wait_ge(ln_loaded, 32 * (l + 1))
                dve.scalar_tensor_tensor(row, row, meanvar[0:n, t, 0:1], ln_g[0:n, :], ALU.subtract, ALU.mult) \
                    .then_inc(dve_step.mark((l, "gain", t)), 1)
                dve.wait_ge(dve_step.sem, dve_step.at((l, "gain", t)))
                dve.wait_ge(rstd_made.sem, rstd_made.at(step))
                out = dve.scalar_tensor_tensor(row, row, rstd[0:n, t:t + 1], ln_b[0:n, :], ALU.mult, ALU.add)
                out.then_inc(normed.mark((l, "x" if l < DEPTH - 1 else "h", t)), 1)

            def second_input(t):
                l = DEPTH - 1
                dve.wait_ge(normed.sem, normed.at((l, "h", t)))
                if t > 2:
                    dve.wait_ge(psum_full.sem, psum_full.at((l, "xT", t - 2)))
                dve.wait_ge(rstd_made.sem, rstd_made.at((2, "in", t)))
                dve.wait_ge(gain_loaded, 16)
                dve.scalar_tensor_tensor(hn[t % 2][:, :], h[:, t, :], rstd[:, 8 + t:9 + t], gain[:, :], ALU.mult, ALU.mult) \
                    .then_inc(normed.mark((l, "x", t)), 1)

            def x_lo(l, t):
                use = (l, "xT", t)
                n = SIZE[t]
                dve.wait_ge(hi_made.sem, hi_made.at((l, "x", t)))
                src = psum(use)[:, :, :].rearrange("p a (k n) -> p (a k) n", n=P)[:, :, 0:n]
                dve.tensor_tensor(xlo[:, :, START[t]:END[t]], src, xhi[:, :, START[t]:END[t]].bitcast(F32),
                                  ALU.subtract).then_inc(dve_took.mark(use), 1)

            for c in range(4):
                dve.wait_ge(hi_made.sem, hi_made.at((0, "x0", c)))
                dve.tensor_tensor(xlo[:, 2 * c:2 * c + 2, :], xt0[:, 2 * c:2 * c + 2, :],
                                  xhi[:, 2 * c:2 * c + 2, :].bitcast(F32), ALU.subtract) \
                    .then_inc(lo_made.mark((0, "x0", c)), 1)
                if c < 2:
                    a, b = c * BLOCK // 2, (c + 1) * BLOCK // 2
                    dve.wait_ge(hi_made.sem, hi_made.at((0, "w0", c)))
                    dve.tensor_tensor(wlo[0][:, a:b], raw[0][:, a:b], whi[0][:, a:b].bitcast(F32), ALU.subtract) \
                        .then_inc(lo_made.mark((0, "w0", c)), 1)
            dve.wait_ge(consts_loaded, 64)
            dve.wait_ge(set_up.sem, set_up.at("mask0"))
            for l in range(DEPTH):
                gate_conv_input(l, 0)
                gate_conv_input(l, 1)
                conv(l, 0, 0, 17)
                gate_conv_input(l, 2)
                gate_conv_input(l, 3)
                conv(l, 0, 17, TAPS)
                for c in range(CT):
                    rope(l, "qi", c)
                rope(l, "ki", 0)
                cuts = [0] + [TAPS_AHEAD * (g + 1) // 4 for g in range(4)]
                for g in range(4):
                    conv(l, 2, cuts[g], cuts[g + 1])
                    add_scores(l, 2 * g)
                    add_scores(l, 2 * g + 1)
                todo = [(name, c) for name in ("q", "k") for c in range(CT)]
                topk(l, lambda r: rope(l, *todo.pop(0)) if r >= 2 and (r - 2) % 3 < 2 and todo else None)
                for name, c in todo:
                    rope(l, name, c)
                first, todo = extras[l]["dve_first"], extras[l]["dve"]
                n = len(items[l])
                masked_logits(l, 0)
                masked_logits(l, 1)
                for i in range(n):
                    for op in first[i]:
                        y_part(l, *op[1:])
                    normalise(l, i)
                    if i + 2 < n:
                        masked_logits(l, i + 2)
                    for op in todo[i]:
                        if op[0] == "za":
                            gate(l, *op[1:])
                        elif op[0] == "taps":
                            conv(l, 2, *op[1:])
                        elif op[0] == "stats":
                            conv_stats(l, op[1])
                        elif op[0] == "norm":
                            conv_norm(l, op[1])
                        else:
                            y_part(l, *op[1:])
                y_part(l, "attn", 4)
                tiles = list(query_tiles(l))
                for t in tiles:
                    residual(l, 0, t)
                for t in tiles:
                    residual(l, 1, t)
                    post_norm(l, t)
                    if l < DEPTH - 1:
                        if t - 1 in tiles:
                            x_lo(l, t - 1)
                    else:
                        if t - 1 in tiles:
                            second_input(t - 1)
                        if t - 2 in tiles:
                            x_lo(l, t - 2)
                if l == DEPTH - 1:
                    second_input(4)
                    x_lo(l, 3)
                x_lo(l, 4)

            dve.wait_ge(block2_loaded, 8 * 16)

            def gained_tables(dst_c, dst_s, g, factor, name):
                gb = g[:, :].rearrange("p (o d) -> p o d", o=1).broadcast_to([P, 4, HD])
                dve.scalar_tensor_tensor(dst_c[:, :, :], c2[:, :, :], factor, gb, ALU.mult, ALU.mult) \
                    .then_inc(dve_step.mark((2, name, "c")), 1)
                for half in range(2):
                    for s in range(2):
                        a, b = half * AXIAL + s * 16, half * AXIAL + (1 - s) * 16
                        gp = g[:, b:b + 16].rearrange("p (o d) -> p o d", o=1).broadcast_to([P, 4, 16])
                        got = dve.scalar_tensor_tensor(dst_s[:, :, a:a + 16], s2[:, :, a:a + 16], factor, gp,
                                                       ALU.mult, ALU.mult)
                        got.then_inc(dve_step.mark((2, name, half, s)), 1)

            gained_tables(gcq, gsq, qg, SCALE, "q")
            gained_tables(gck, gsk, kg, 1.0, "k")

            def qk_squares(t, name):
                h0, h1 = (0, HEADS) if name == "q" else (HEADS, HEADS + 2)
                row, step = qrow[t][:, h0:h1, :], (2, name + "sq", t)
                dve.wait_ge(act_took.sem, act_took.at((2, "q" if name == "q" else "kv", t)))
                if t:
                    dve.wait_ge(stats_made.sem, stats_made.at((2, name, t - 1)))
                dve.tensor_tensor(qtmp[:, h0:h1, :], row, row, ALU.mult).then_inc(dve_step.mark(step), 1)
                dve.wait_ge(dve_step.sem, dve_step.at(step))
                dve.tensor_reduce(squares[:, t, h0:h1], qtmp[:, h0:h1, :], mybir.AxisListType.X, ALU.add) \
                    .then_inc(stats_made.mark((2, name, t)), 1)

            def qk_rows(t):
                row, rot = qrow[t], qrot[t]
                dve.wait_ge(rstd_made.sem, rstd_made.at((2, "q", t)))
                dve.wait_ge(rstd_made.sem, rstd_made.at((2, "k", t)))
                r = unit[:, t, :].rearrange("p (h o) -> p h o", o=1).broadcast_to([P, 10, HD])
                dve.tensor_tensor(row[:, :, :], row[:, :, :], r, ALU.mult).then_inc(dve_step.mark((2, "unit", t)), 1)
                dve.wait_ge(dve_step.sem, dve_step.at((2, "unit", t)))
                dve.wait_ge(stats_made.sem, stats_made.at((2, "k", 3)))
                if t:
                    dve.wait_ge(normed.sem, normed.at((2, "rope", t - 1)))
                for h0, h1, gc, gs in ((0, 8, gcq, gsq), (8, 10, gck, gsk)):
                    nh = h1 - h0
                    cb = gc[:, t, :].rearrange("p (o d) -> p o d", o=1).broadcast_to([P, nh, HD])
                    dve.tensor_tensor(rot[:, h0:h1, :], row[:, h0:h1, :], cb, ALU.mult)
                    for half in range(2):
                        for s in range(2):
                            a, b = half * AXIAL + s * 16, half * AXIAL + (1 - s) * 16
                            sb_ = gs[:, t, a:a + 16].rearrange("p (o d) -> p o d", o=1).broadcast_to([P, nh, 16])
                            got = dve.tensor_tensor(qtmp[:, h0:h1, a:a + 16], row[:, h0:h1, b:b + 16], sb_, ALU.mult)
                got.then_inc(normed.mark((2, "qk", t)), 1)
                dve.wait_ge(normed.sem, normed.at((2, "qk", t)))
                dve.tensor_tensor(rot[:, :, :], rot[:, :, :], qtmp[:, :, :], ALU.add).then_inc(normed.mark((2, "rope", t)), 1)

            def v_rows(t):
                step = (2, "v", t)
                row = vv[:, t, :]
                dve.wait_ge(act_took.sem, act_took.at((2, "vin", t)))
                dve.bn_stats(stats[:, t, 0, :], row).then_inc(dve_step.mark(step), 1)
                dve.wait_ge(dve_step.sem, dve_step.at(step))
                dve.bn_aggr(meanvar[:, t, :], stats[:, t, 0, :]).then_inc(stats_made.mark(step), 1)
                dve.wait_ge(stats_made.sem, stats_made.at(step))
                dve.scalar_tensor_tensor(row, row, meanvar[:, t, 0:1], lnv_g[:, :], ALU.subtract, ALU.mult) \
                    .then_inc(dve_step.mark((2, "vg", t)), 1)
                dve.wait_ge(dve_step.sem, dve_step.at((2, "vg", t)))
                dve.wait_ge(rstd_made.sem, rstd_made.at(step))
                dve.scalar_tensor_tensor(row, row, rstd[:, 12 + t:13 + t], lnv_b[:, :], ALU.mult, ALU.add) \
                    .then_inc(normed.mark(step), 1)

            def qk_lo(t):
                use = (2, "qkT", t)
                ps = psum(use)
                dve.wait_ge(hi_made.sem, hi_made.at(use))
                for odd in range(2):
                    part, other = slice(HD * odd, HD * odd + HD), slice(HD - HD * odd, P - HD * odd)
                    tile = q2[t // 2][:, :, t % 2, odd, :]
                    dve.tensor_tensor(tile[other], ps[part, 0, :].rearrange("p (c n) -> p c n", n=P),
                                      tile[part].bitcast(F32), ALU.subtract)
                for g in range(2):
                    part = slice(HD * g, HD * g + HD)
                    for s in range(2):
                        got = dve.tensor_tensor(k2_lo[HD * s:HD * s + HD, g, P * t:P * t + P], ps[part, 1, 0:P],
                                                k2_hi[part, g, P * t:P * t + P].bitcast(F32), ALU.subtract)
                got.then_inc(dve_took.mark(use), 1)

            def u_rows(t):
                dve.wait_ge(act_took.sem, act_took.at((2, "gb", t)))
                dve.wait_ge(act_took.sem, act_took.at((2, "u", t)))
                dve.tensor_tensor(ug[:, t, :], ug[:, t, :], sgb[t][:, :], ALU.mult).then_inc(normed.mark((2, "ug", t)), 1)

            def mlp_gate(pair_):
                use = (2, "vmix", pair_)
                ps = full(use)
                dve.wait_ge(normed.sem, normed.at((2, "ug", 3)))
                for i in range(2):
                    g = 2 * pair_ + i
                    dst = ug[:, :, g * GD:g * GD + GD]
                    got = dve.scalar_tensor_tensor(dst, ps[:, i, 0:4 * GD].rearrange("p (t d) -> p t d", t=4),
                                                   vec[:, V_BSPAT + g:V_BSPAT + g + 1], dst, ALU.add, ALU.mult)
                got.then_inc(dve_took.mark(use), 1)

            def mlp_low(t):
                use = (2, "gmT", t)
                dve.wait_ge(hi_made.sem, hi_made.at((2, "gm", t)))
                c0, c1 = P * t, P * t + P
                dve.tensor_tensor(mlp_lo[:, :, c0:c1], psum(use)[:, 0, :].rearrange("p (c n) -> p c n", n=P),
                                  mlp_hi[:, :, c0:c1].bitcast(F32), ALU.subtract).then_inc(dve_took.mark(use), 1)

            def max2(i):
                t, hd = items2[i]
                ps = full((2, "S2", t, hd))
                if i >= 4:
                    dve.wait_ge(act_took.sem, act_took.at((2, "S2", *items2[i - 4])))
                dve.tensor_reduce(nmax[:, i % 4:i % 4 + 1], ps[:, 0, :], mybir.AxisListType.X, ALU.max, negate=True) \
                    .then_inc(rsum_made.mark((2, "max", i)), 1)

            def normalise2(i):
                t, hd = items2[i]
                dve.wait_ge(act_took.sem, act_took.at((2, "S2", t, hd)))
                dve.reciprocal(rsums[:, i % 4:i % 4 + 1], psums[:, i % 4:i % 4 + 1]).then_inc(rsum_made.mark((2, i)), 1)
                dve.wait_ge(rsum_made.sem, rsum_made.at((2, i)))
                dve.tensor_scalar(e2[i % 3][:, :], e2[i % 3][:, :], rsums[:, i % 4:i % 4 + 1], None, ALU.mult) \
                    .then_inc(probs_made.mark((2, i)), 1)

            def attn2_part(t):
                use = (2, "O2", t)
                dve.wait_ge(psum_full.sem, psum_full.at((2, "PV2", t, HEADS - 1)))
                if t >= 2:
                    dve.wait_ge(lo_made.sem, lo_made.at((2, "attn", t - 2)))
                dve.tensor_tensor(yt2[t % 2][:, :].rearrange("p (c n) -> p c n", n=P),
                                  psum(use)[:, 0, :].rearrange("p (c n) -> p c n", n=P),
                                  sga[:, :, P * t:P * t + P], ALU.mult).then_inc(y_made.mark((2, "attn", t)), 1)

            def attn2_lo(t):
                dve.wait_ge(hi_made.sem, hi_made.at((2, "attn", t)))
                c0, c1 = P * t, P * t + P
                dve.tensor_tensor(attn_lo[:, :, c0:c1], yt2[t % 2][:, :].rearrange("p (c n) -> p c n", n=P),
                                  attn_hi[:, :, c0:c1].bitcast(F32), ALU.subtract).then_inc(lo_made.mark((2, "attn", t)), 1)

            def merge(d):
                for name, c in (("yb", KD + d), ("ya", d)):
                    use = (2, name, d)
                    dve.scalar_tensor_tensor(tg[:, c, :], tg[:, c, :], 1.0, full(use)[:, 0, :], ALU.add, ALU.mult) \
                        .then_inc(dve_took.mark(use), 1)
                dve.wait_ge(dve_took.sem, dve_took.at((2, "ya", d)))
                if d >= 2:
                    dve.wait_ge(lo_made.sem, lo_made.at((2, "y", d - 2)))
                dve.tensor_tensor(yt2[d % 2][:, :], tg[:, d, :], tg[:, KD + d, :], ALU.add).then_inc(y_made.mark((2, "y", d)), 1)

            def merge_lo(d):
                dve.wait_ge(hi_made.sem, hi_made.at((2, "y", d)))
                dve.tensor_tensor(xlo[:, d, 0:SEQ], yt2[d % 2][:, :], xhi[:, d, 0:SEQ].bitcast(F32), ALU.subtract) \
                    .then_inc(lo_made.mark((2, "y", d)), 1)

            def last_residual(half, t):
                use = (2, "wo", half, t)
                ps = full(use)
                dst = h[:, t + 1, half * 512:half * 512 + 512]
                dve.scalar_tensor_tensor(dst, ps[:, 0, :], 0.5, dst, ALU.mult, ALU.add).then_inc(dve_took.mark(use), 1)

            def last_norm(t):
                dve.wait_ge(rstd_made.sem, rstd_made.at(("out", t)))
                dve.scalar_tensor_tensor(h[:, t + 1, :], h[:, t + 1, :], rstd[:, t:t + 1], fgain[:, :], ALU.mult, ALU.mult) \
                    .then_inc(normed.mark(("out", t)), 1)

            for name in ("q", "k"):
                for t in range(4):
                    qk_squares(t, name)
            for t in range(4):
                qk_rows(t)
            for t in range(4):
                v_rows(t)
            for t in range(4):
                qk_lo(t)
            for t in range(4):
                u_rows(t)
            for pair_ in range(4):
                mlp_gate(pair_)
            n = len(items2)
            max2(0)
            max2(1)
            for i in range(n):
                normalise2(i)
                if i > 1 and i % HEADS == 1:
                    attn2_part(i // HEADS - 1)
                if i + 2 < n:
                    max2(i + 2)
                if i % 2 and i < 8:
                    mlp_low(i // 2)
                if i > 2 and i % HEADS == 2:
                    attn2_lo(i // HEADS - 1)
            attn2_part(3)
            attn2_lo(3)
            for d in range(KD):
                merge(d)
                if d:
                    merge_lo(d - 1)
            merge_lo(KD - 1)
            for t in range(4):
                last_residual(0, t)
            for t in range(4):
                last_residual(1, t)
                if t:
                    last_norm(t - 1)
            last_norm(3)

        out = {name: s.steps for name, s in signals.items()}
        out["psum"] = psum_of
    return out


def rope_tables():
    freq = np.float32(THETA) ** (-np.arange(0, HD, 2, dtype=np.float32) / np.float32(HD))
    ang = np.arange(L, dtype=np.float32)[:, None] * freq[None, :]
    c, s = np.cos(ang).T, np.sin(ang).T
    return (np.ascontiguousarray(np.concatenate([c, c, c, c], 0), np.float32),
            np.ascontiguousarray(np.concatenate([-s, s, -s, s], 0), np.float32))


def axial_tables():
    freq = np.float32(THETA) ** (-np.arange(0, AXIAL, 2, dtype=np.float32) / np.float32(AXIAL))
    pos = np.arange(SEQ)
    parts_c, parts_s = [], []
    for where in (pos // GRID_W, pos % GRID_W):
        ang = where.astype(np.float32)[:, None] * freq[None, :]
        c, s = np.cos(ang), np.sin(ang)
        parts_c += [c, c]
        parts_s += [-s, s]
    c, s = (np.concatenate(x, 1).astype(np.float32).reshape(4, P, HD).transpose(1, 0, 2) for x in (parts_c, parts_s))
    return np.ascontiguousarray(c), np.ascontiguousarray(s)


def column_block(w, c0, width):
    out = np.zeros((P, BLOCK), w.dtype)
    out[:, 0:KD * width] = w[:, c0:c0 + width].reshape(KD, P, width).transpose(1, 0, 2).reshape(P, KD * width)
    return out


def half_block(w, half, c0):
    return w[half * 512:half * 512 + 512, c0:c0 + 512].reshape(4, P, 512).transpose(1, 0, 2).reshape(P, BLOCK)


def pack_weights(i):
    sizes = [512, 512, 512, 512, 512, 512, 512, 512, 64, 8]
    names = ["a", "g", "zc", "q", "k", "v", "za", "qi", "ki", "wi"]
    at = dict(zip(names, np.cumsum([0] + sizes)))
    names2 = ["q", "kv", "ga", "u", "vin", "gb", "gm"]
    at2 = dict(zip(names2, np.cumsum([0, 512, 256, 512, 512, 512, 512])))
    out = np.empty((len(BLOCKS), P, BLOCK), np.asarray(i["w_in"]).dtype)
    for n, (key, _, _) in enumerate(BLOCKS):
        l, name, x = key[0], key[1], key[2]
        if l < DEPTH:
            w = i["w_in"][l]
            if name == "wo":
                out[n] = half_block(i["w_out"][l], key[3], 512 * x)
            elif name == "v":
                out[n] = half_block(w, x, at["v"])
            elif name == "ki":
                out[n] = column_block(w, at["ki"], HD + HEADS)
            else:
                out[n] = column_block(w, at[name] + P * x, 2 * P)
        else:
            w = i["w_in_2"][0]
            if name == "wo":
                out[n] = half_block(i["w_out_2"][0], key[3], 512 * x)
            elif name in ("ya", "yb"):
                out[n] = half_block(i["w_proj_attn_2" if name == "ya" else "w_proj_gmlp_2"][0], 0, P * x)
            elif name in ("q", "vin", "u", "gb"):
                out[n] = half_block(w, x, at2[name])
            else:
                out[n] = column_block(w, at2[name] + P * x, 2 * P)
    return out


def pack_vectors(i):
    rows = [np.asarray(i["conv_w"]).reshape(-1, P)]
    for name in ("conv_b", "conv_ln_g", "conv_ln_b"):
        rows.append(np.asarray(i[name]).reshape(-1, P))
    rows.append(np.asarray(i["b_merge_2"]).reshape(-1, P))
    rows.append(np.asarray(i["b_spatial_2"]).reshape(-1, P))
    return np.ascontiguousarray(np.concatenate(rows, 0).T)


def kernel(**inputs):
    import concourse.bacc as bacc
    from concourse.bass_utils import run_bass_kernel_spmd as run

    i = {name: np.asarray(a) for name, a in inputs.items()}
    rope_cos, rope_sin = rope_tables()
    axial_cos, axial_sin = axial_tables()
    rows = np.concatenate([i["meta_tokens"], i["x"][0]], 0)
    arrays = {
        "weights": pack_weights(i),
        "vectors": pack_vectors(i),
        "x_t": np.ascontiguousarray(rows.T.reshape(KD, P, L).transpose(1, 0, 2)),
        "w_spatial_t": np.ascontiguousarray(i["w_spatial_2"][0].transpose(2, 0, 1)),
        "identity": np.eye(P, dtype=np.float32),
        "rope_cos": rope_cos, "rope_sin": rope_sin, "axial_cos": axial_cos, "axial_sin": axial_sin,
    }
    for name in ("x", "meta_tokens", "post_ln_g", "post_ln_b", "norm_gain_2", "q_gain_2", "k_gain_2",
                 "ln_v_gain_2", "ln_v_bias_2", "final_gain_2"):
        arrays[name] = np.ascontiguousarray(i[name])

    def program(counted):
        nc = bacc.Bacc("TRN2", target_bir_lowering=False, num_devices=1, dynamic_dma_scratch_size=1024)
        io = {name: nc.dram_tensor(f"in_{name}", a.shape, mybir.dt.from_np(a.dtype), kind="ExternalInput").ap()
              for name, a in arrays.items()}
        io["out"] = nc.dram_tensor("out_0", (1, SEQ, D), F32, kind="ExternalOutput").ap()
        return nc, build(nc, io, counted)

    _, counted = program(None)
    nc, again = program(counted)
    assert again == counted
    r = run(nc, [{f"in_{name}": a for name, a in arrays.items()}], core_ids=[0])
    return r.results[0]["out_0"]
```
